# Optimizing a Trainium2 kernel written in Bass

```python
import functools
import jax, jax.numpy as jnp
from jax import lax
import numpy as np

D_MODEL = 1024
BATCH = 1
SEQ = 1024
DEPTH = 1
DEC_BATCH = 1
DEC_SEQ = 64
PAST_LEN = 512

CHUNK = 64
Q_BLOCK = 128
H_FOX = 8
HD_FOX = 64
D_FOX = H_FOX * HD_FOX
D_CONV = 512
CONV_WIDTH = 31
CONV_STATE = CONV_WIDTH - 1
H_MEM = 4
HD_MEM = 128
D_MEM = H_MEM * HD_MEM
N_MEM = 256
N_BRANCH = 3
PEER_HEADS = 8
PEER_NKEYS = 128
PEER_N = PEER_NKEYS * PEER_NKEYS
PEER_DK = 256
PEER_TOPK = 16
PEER_TOK_BLOCK = 128
EPS = 1e-6

OFF_Q = 0
OFF_K = OFF_Q + D_FOX
OFF_V = OFF_K + D_FOX
OFF_F = OFF_V + D_FOX
OFF_GLU = OFF_F + H_FOX
OFF_MQ = OFF_GLU + 2 * D_CONV
OFF_G = OFF_MQ + D_MEM
IN_COLS = OFF_G + N_BRANCH * D_MODEL

kernel_name = 'fox_conformer_memory_peer_stream_step'

def rmsnorm(x, w):
    xf = x.astype(jnp.float32)
    xf = xf * lax.rsqrt(jnp.mean(xf * xf, axis=-1, keepdims=True) + EPS)
    return (xf * w.astype(jnp.float32)).astype(x.dtype)

def layernorm(x, w, b):
    xf = x.astype(jnp.float32)
    mu = jnp.mean(xf, axis=-1, keepdims=True)
    xc = xf - mu
    var = jnp.mean(xc * xc, axis=-1, keepdims=True)
    out = xc * lax.rsqrt(var + EPS) * w.astype(jnp.float32) + b.astype(jnp.float32)
    return out.astype(x.dtype)

def project_in(x, norm_w, w_in, b_f):
    N, T = x.shape[:2]
    z = rmsnorm(x, norm_w) @ w_in
    q = z[..., OFF_Q:OFF_K].reshape(N, T, H_FOX, HD_FOX)
    k = z[..., OFF_K:OFF_V].reshape(N, T, H_FOX, HD_FOX)
    v = z[..., OFF_V:OFF_F].reshape(N, T, H_FOX, HD_FOX)
    logf = jax.nn.log_sigmoid((z[..., OFF_F:OFF_GLU] + b_f).astype(jnp.float32))
    glu = z[..., OFF_GLU:OFF_MQ]
    a = glu[..., :D_CONV] * jax.nn.sigmoid(glu[..., D_CONV:])
    mq = z[..., OFF_MQ:OFF_G].reshape(N, T, H_MEM, HD_MEM)
    gates = jax.nn.sigmoid(z[..., OFF_G:].reshape(N, T, N_BRANCH, D_MODEL))
    return q, k, v, logf, a, mq, gates

def fox_block(qb, k, v, q_term, k_term, q_pos, k_pos):
    s = jnp.einsum('nqhd,nkhd->nhqk', qb, k).astype(jnp.float32) * (HD_FOX ** -0.5)
    bias = jnp.swapaxes(q_term, 1, 2)[..., :, None] + jnp.swapaxes(k_term, 1, 2)[..., None, :]
    mask = k_pos[None, :] <= q_pos[:, None]
    s = jnp.where(mask, s + bias, -jnp.inf)
    p = jax.nn.softmax(s, axis=-1).astype(v.dtype)
    return jnp.einsum('nhqk,nkhd->nqhd', p, v)

def fox_prompt(q, k, v, logf):
    N, T = q.shape[:2]
    c = jnp.cumsum(logf, axis=1)
    nb = T // Q_BLOCK
    pos = jnp.arange(T)
    qb = jnp.swapaxes(q.reshape(N, nb, Q_BLOCK, H_FOX, HD_FOX), 0, 1)
    cb = jnp.swapaxes(c.reshape(N, nb, Q_BLOCK, H_FOX), 0, 1)
    pb = pos.reshape(nb, Q_BLOCK)
    out = lax.map(lambda blk: fox_block(blk[0], k, v, blk[1], -c, blk[2], pos), (qb, cb, pb))
    return jnp.swapaxes(out, 0, 1).reshape(N, T, H_FOX, HD_FOX)

def fox_sample(q, k, v, logf, ck, cv, clogf):
    P = ck.shape[1]
    S = q.shape[1]
    clogf = clogf.astype(jnp.float32)
    cnew = jnp.cumsum(logf, axis=1)
    suffix = lax.cumsum(clogf, axis=1, reverse=True) - clogf
    k_term = jnp.concatenate([suffix, -cnew], axis=1)
    keys = jnp.concatenate([ck.astype(k.dtype), k], axis=1)
    vals = jnp.concatenate([cv.astype(v.dtype), v], axis=1)
    return fox_block(q, keys, vals, cnew, k_term, P + jnp.arange(S), jnp.arange(P + S))

def conv_branch(a, hist, w_dw, b_dw, ln_w, ln_b, w_o):
    full = jnp.concatenate([hist.astype(a.dtype), a], axis=1)
    y = lax.conv_general_dilated(full, w_dw[:, None, :], window_strides=(1,), padding='VALID',
                                 dimension_numbers=('NWC', 'WIO', 'NWC'),
                                 feature_group_count=D_CONV) + b_dw
    y = jax.nn.silu(layernorm(y, ln_w, ln_b))
    return y @ w_o, full[:, -CONV_STATE:]

def mem_kv(mem, norm_w, w_kv, k_norm_w):
    N, M = mem.shape[:2]
    m = rmsnorm(mem, norm_w) @ w_kv
    mk = rmsnorm(m[..., :D_MEM].reshape(N, M, H_MEM, HD_MEM), k_norm_w)
    mv = m[..., D_MEM:].reshape(N, M, H_MEM, HD_MEM)
    return mk, mv

def mem_branch(mq, mk, mv, w_o):
    N, T = mq.shape[:2]
    s = jnp.einsum('nqhd,nkhd->nhqk', mq, mk.astype(mq.dtype)).astype(jnp.float32) * (HD_MEM ** -0.5)
    p = jax.nn.softmax(s, axis=-1).astype(mq.dtype)
    o = jnp.einsum('nhqk,nkhd->nqhd', p, mv.astype(mq.dtype))
    return o.reshape(N, T, D_MEM) @ w_o

def peer(h, w_q, keys1, keys2, u, v):
    N, T, D = h.shape
    n = N * T
    nb = -(-n // PEER_TOK_BLOCK)
    flat = jnp.pad(h.reshape(n, D), ((0, nb * PEER_TOK_BLOCK - n), (0, 0)))

    def block(xb):
        B = xb.shape[0]
        q = (xb @ w_q).reshape(B, PEER_HEADS, 2, PEER_DK // 2)
        s1 = jnp.einsum('bhd,hkd->bhk', q[:, :, 0], keys1).astype(jnp.float32)
        s2 = jnp.einsum('bhd,hkd->bhk', q[:, :, 1], keys2).astype(jnp.float32)
        v1, i1 = lax.top_k(s1, PEER_TOPK)
        v2, i2 = lax.top_k(s2, PEER_TOPK)
        cand = (v1[..., :, None] + v2[..., None, :]).reshape(B, PEER_HEADS, PEER_TOPK * PEER_TOPK)
        cidx = (i1[..., :, None] * PEER_NKEYS + i2[..., None, :]).reshape(B, PEER_HEADS, PEER_TOPK * PEER_TOPK)
        top, pos = lax.top_k(cand, PEER_TOPK)
        idx = jnp.take_along_axis(cidx, pos, axis=-1)
        g = jax.nn.softmax(top, axis=-1).astype(xb.dtype)
        ue = u[idx]
        ve = v[idx]
        act = jax.nn.gelu(jnp.einsum('bd,bhkd->bhk', xb, ue), approximate=False)
        return jnp.einsum('bhk,bhkd->bd', g * act, ve)

    out = lax.map(block, flat.reshape(nb, PEER_TOK_BLOCK, D))
    return out.reshape(nb * PEER_TOK_BLOCK, D)[:n].reshape(N, T, D)

def layer(x, conv_hist, mk, mv, fox_fn, w):
    N, T = x.shape[:2]
    q, k, v, logf, a, mq, gates = project_in(x, w['norm1'], w['w_in'], w['b_f'])
    q = rmsnorm(q, w['fox_qn'])
    k = rmsnorm(k, w['fox_kn'])
    o_fox = fox_fn(q, k, v, logf).reshape(N, T, D_FOX) @ w['w_fox_o']
    o_conv, conv_state = conv_branch(a, conv_hist, w['w_dw'], w['b_dw'], w['ln_w'], w['ln_b'], w['w_conv_o'])
    o_mem = mem_branch(rmsnorm(mq, w['mem_qn']), mk, mv, w['w_mem_o'])
    merged = gates[:, :, 0] * o_fox + gates[:, :, 1] * o_conv + gates[:, :, 2] * o_mem
    x = x + merged @ w['w_out']
    x = x + peer(rmsnorm(x, w['norm2']), w['pq'], w['pk1'], w['pk2'], w['pu'], w['pv'])
    return x, k, v, logf, conv_state

def setup_inputs(seed: int = 0) -> dict:
    key = jax.random.key(seed)
    ks = iter(jax.random.split(key, 40))

    def nrm(shape, scale):
        return jax.random.normal(next(ks), shape, jnp.float32) * scale

    def gain(shape):
        return 1.0 + nrm(shape, 0.05)

    L = DEPTH
    return {
        'x_prompt': nrm((BATCH, SEQ, D_MODEL), 1.0),
        'x_sample': nrm((DEC_BATCH, DEC_SEQ, D_MODEL), 1.0),
        'mem_prompt': nrm((BATCH, N_MEM, D_MODEL), 1.0),
        'cache_fox_k': nrm((L, DEC_BATCH, PAST_LEN, H_FOX, HD_FOX), 1.0),
        'cache_fox_v': nrm((L, DEC_BATCH, PAST_LEN, H_FOX, HD_FOX), 1.0),
        'cache_fox_logf': jax.nn.log_sigmoid(2.5 + nrm((L, DEC_BATCH, PAST_LEN, H_FOX), 0.5)),
        'cache_conv': nrm((L, DEC_BATCH, CONV_STATE, D_CONV), 0.5),
        'cache_mem_k': nrm((L, DEC_BATCH, N_MEM, H_MEM, HD_MEM), 1.0),
        'cache_mem_v': nrm((L, DEC_BATCH, N_MEM, H_MEM, HD_MEM), 1.0),
        'norm1_w': gain((L, D_MODEL)),
        'w_in': nrm((L, D_MODEL, IN_COLS), D_MODEL ** -0.5),
        'b_forget': 2.5 + nrm((L, H_FOX), 0.5),
        'fox_q_norm': gain((L, HD_FOX)),
        'fox_k_norm': gain((L, HD_FOX)),
        'w_fox_o': nrm((L, D_FOX, D_MODEL), D_FOX ** -0.5),
        'w_dw': nrm((L, CONV_WIDTH, D_CONV), CONV_WIDTH ** -0.5),
        'b_dw': nrm((L, D_CONV), 0.02),
        'conv_ln_w': gain((L, D_CONV)),
        'conv_ln_b': nrm((L, D_CONV), 0.02),
        'w_conv_o': nrm((L, D_CONV, D_MODEL), D_CONV ** -0.5),
        'mem_norm_w': gain((L, D_MODEL)),
        'w_mem_kv': nrm((L, D_MODEL, 2 * D_MEM), D_MODEL ** -0.5),
        'mem_q_norm': gain((L, HD_MEM)),
        'mem_k_norm': gain((L, HD_MEM)),
        'w_mem_o': nrm((L, D_MEM, D_MODEL), D_MEM ** -0.5),
        'w_out': nrm((L, D_MODEL, D_MODEL), D_MODEL ** -0.5),
        'norm2_w': gain((L, D_MODEL)),
        'peer_w_q': nrm((L, D_MODEL, PEER_HEADS * PEER_DK), D_MODEL ** -0.5),
        'peer_keys1': nrm((L, PEER_HEADS, PEER_NKEYS, PEER_DK // 2), (PEER_DK // 2) ** -0.5),
        'peer_keys2': nrm((L, PEER_HEADS, PEER_NKEYS, PEER_DK // 2), (PEER_DK // 2) ** -0.5),
        'peer_u': nrm((L, PEER_N, D_MODEL), D_MODEL ** -0.5),
        'peer_v': nrm((L, PEER_N, D_MODEL), 0.3),
    }

def reference(x_prompt, x_sample, mem_prompt, cache_fox_k, cache_fox_v, cache_fox_logf, cache_conv,
              cache_mem_k, cache_mem_v, norm1_w, w_in, b_forget, fox_q_norm, fox_k_norm, w_fox_o,
              w_dw, b_dw, conv_ln_w, conv_ln_b, w_conv_o, mem_norm_w, w_mem_kv, mem_q_norm, mem_k_norm,
              w_mem_o, w_out, norm2_w, peer_w_q, peer_keys1, peer_keys2, peer_u, peer_v):
    xp = x_prompt
    xs = x_sample
    pk, pv, pf, pc, pmk, pmv = [], [], [], [], [], []
    sk, sv, sf, sc = [], [], [], []
    for l in range(DEPTH):
        w = dict(norm1=norm1_w[l], w_in=w_in[l], b_f=b_forget[l], fox_qn=fox_q_norm[l], fox_kn=fox_k_norm[l],
                 w_fox_o=w_fox_o[l], w_dw=w_dw[l], b_dw=b_dw[l], ln_w=conv_ln_w[l], ln_b=conv_ln_b[l],
                 w_conv_o=w_conv_o[l], mem_qn=mem_q_norm[l], w_mem_o=w_mem_o[l], w_out=w_out[l],
                 norm2=norm2_w[l], pq=peer_w_q[l], pk1=peer_keys1[l], pk2=peer_keys2[l],
                 pu=peer_u[l], pv=peer_v[l])
        mk_p, mv_p = mem_kv(mem_prompt, mem_norm_w[l], w_mem_kv[l], mem_k_norm[l])
        hist0 = jnp.zeros((xp.shape[0], CONV_STATE, D_CONV), xp.dtype)
        xp, k_p, v_p, f_p, c_p = layer(xp, hist0, mk_p, mv_p, fox_prompt, w)
        pk.append(k_p); pv.append(v_p); pf.append(f_p); pc.append(c_p); pmk.append(mk_p); pmv.append(mv_p)
        fox_s = functools.partial(fox_sample, ck=cache_fox_k[l], cv=cache_fox_v[l], clogf=cache_fox_logf[l])
        xs, k_s, v_s, f_s, c_s = layer(xs, cache_conv[l], cache_mem_k[l], cache_mem_v[l], fox_s, w)
        sk.append(k_s); sv.append(v_s); sf.append(f_s); sc.append(c_s)
    return (xp, xs,
            jnp.stack(pk), jnp.stack(pv), jnp.stack(pf), jnp.stack(pc), jnp.stack(pmk), jnp.stack(pmv),
            jnp.stack(sk), jnp.stack(sv), jnp.stack(sf), jnp.stack(sc))


_drawn_inputs = setup_inputs


def setup_inputs(seed=0):
    import zlib

    import numpy as np

    out = dict(_drawn_inputs(seed))
    spreads = {}
    factors = {'cache_fox_logf': 21.532,
     'fox_q_norm': 4.113,
     'b_dw': 2.803,
     'conv_ln_b': 4.258,
     'mem_q_norm': 7.335}
    for name, (base, spread) in spreads.items():
        noise = np.random.default_rng([zlib.crc32(name.encode()), seed]).standard_normal(out[name].shape)
        drawn = base * np.exp(spread * noise) if base else spread * noise
        out[name] = __import__('jax').numpy.asarray(drawn.astype(out[name].dtype))
    for name, factor in factors.items():
        out[name] = (out[name] * factor).astype(out[name].dtype)
    return out
```

```python
from contextlib import ExitStack

import concourse.bass as bass
from concourse import mybir

F32 = mybir.dt.float32
U32 = mybir.dt.uint32
ALU = mybir.AluOpType
ACT = mybir.ActivationFunctionType
AX = mybir.AxisListType.X

P = 128
D = 1024
KC = D // P
SEQ = 1024
NT = SEQ // P
SAM = 64
SAMPLE = NT
PAST = 512
TOK = SEQ + P
HF, DF = 8, 64
HM, DM = 4, 128
NMEM = 256
DC = 512
CT = DC // P
CW = 31
HIST = CW - 1
NH, NK, TOPK = 8, 128, 16
EPS = 1e-6
MASKED = -1e30
LOWEST = -3.4e38
C_GLU = 3 * HF * DF + HF
C_MQ = C_GLU + 2 * DC
C_G = C_MQ + HM * DM
GATES = 3 * D
S0 = 1
BANK = 512
CONV_OUT = SEQ + HIST + SAM


class Tile:

    def __init__(self, u, b, sample=False, last=False):
        self.u, self.b, self.sample, self.last = u, b, sample, last
        self.n = 2 * u + b

    def next(self):
        if self.b == 0:
            return Tile(self.u, 1)
        return Tile(self.u + 1, 0, sample=self.before_sample)

    before_sample = False


def all_tiles(eng, emit):
    with eng.Fori(0, NT // 2 - 1) as u:
        emit(Tile(u, 0))
        emit(Tile(u, 1))
    emit(Tile(NT // 2 - 1, 0))
    end = Tile(NT // 2 - 1, 1)
    end.before_sample = True
    emit(end)
    emit(Tile(NT // 2, 0, sample=True, last=True))


all_tiles.count = NT + 1


def memory_tiles(eng, emit):
    emit(Tile(0, 0))
    emit(Tile(0, 1, last=True))


memory_tiles.count = NMEM // P


class Chain:

    def __init__(self, eng, sem):
        self.eng, self.sem, self.n = eng, sem, 0
        self.taken = 0

    def step(self, ins):
        ins.then_inc(self.sem, 1)
        self.n = self.n + 1
        self.taken += 1
        return ins

    def wait(self):
        self.eng.wait_ge(self.sem, S0 + self.n)

    def link(self, ins):
        self.step(ins)
        self.wait()


class Phase:

    def __init__(self, nc, tag):
        self.nc, self.tag, self.started = nc, tag, []
        self.stack = ExitStack()

    def __enter__(self):
        self.stack.enter_context(self.nc.cleanup_on_exit())
        return self

    def __exit__(self, *a):
        return self.stack.__exit__(*a)

    def sb(self, name, shape, dt=F32):
        return self.stack.enter_context(self.nc.sbuf_tensor(f"{self.tag}_{name}", shape, dt))

    def banks(self, name, n):
        return self.stack.enter_context(self.nc.psum_tensor(f"{self.tag}_{name}_ps", [P, n, BANK], F32))

    def sem(self, name, start=S0):
        sem = self.nc.alloc_semaphore(name=f"{self.tag}_{name}")
        if start:
            self.started.append(sem)
        return sem

    def start(self):
        engines = (self.nc.sync, self.nc.gpsimd, self.nc.scalar, self.nc.tensor, self.nc.vector)
        for k, sem in enumerate(self.started):
            engines[k % len(engines)].sem_inc(sem, S0)
        self.nc.all_engine_barrier()

    def sems(self, name, n, start=S0):
        return [self.sem(f"{name}{i}", start) for i in range(n)]


V_NORM1, V_MEMNORM, V_LNW, V_LNB, V_BDW, V_ROWS = 0, 8, 16, 20, 24, 28


def constants(nc, io, scr, c):
    with Phase(nc, "const") as p:
        rows = p.sb("vec_rows", [V_ROWS, P])
        dw = p.sb("dw_rows", [CW, DC])
        hist = p.sb("hist_rows", [HIST, DC])
        ps = p.banks("ps_const", 3)
        loaded, zeroed, made, turned, kept = (p.sem(n) for n in ("c_loaded", "c_zeroed", "c_made", "c_turned", "c_kept"))
        p.start()
        with nc.Block() as block:
            @block.sync
            def _(sp):
                for at, name, n in ((V_NORM1, "norm1_w", 8), (V_MEMNORM, "mem_norm_w", 8), (V_LNW, "conv_ln_w", 4),
                                    (V_LNB, "conv_ln_b", 4), (V_BDW, "b_dw", 4)):
                    sp.dma_start(rows[at:at + n, :], io[name][0].rearrange("(n p) -> n p", p=P)).then_inc(loaded, 16)
                sp.dma_start(dw[:], io["w_dw"][0]).then_inc(loaded, 16)
                sp.dma_start(hist[:], io["cache_conv"][0, 0]).then_inc(loaded, 16)
                sp.wait_ge(loaded, S0 + 7 * 16)

            @block.gpsimd
            def _(pool):
                pool.memset(c.ident[:], 0.0).then_inc(zeroed, 1)
                pool.memset(c.causal[:], 0.0).then_inc(zeroed, 1)
                pool.wait_ge(zeroed, S0 + 2)
                pool.affine_select(out=c.ident[:], in_=c.ident[:], compare_op=ALU.not_equal, fill=1.0, base=0,
                                   pattern=[[-1, P]], channel_multiplier=1).then_inc(made, 1)
                pool.affine_select(out=c.causal[:], in_=c.causal[:], compare_op=ALU.is_ge, fill=MASKED, base=0,
                                   pattern=[[-1, P]], channel_multiplier=1).then_inc(made, 1)

            @block.tensor
            def _(pe):
                pe.wait_ge(loaded, S0 + 7 * 16)
                pe.wait_ge(made, S0 + 1)
                pe.transpose(ps[:, 0, 0:V_ROWS], rows[:], c.ident[0:V_ROWS, 0:V_ROWS]).then_inc(turned, 1)
                for j in range(CT):
                    pe.transpose(ps[:, 1, j * CW:(j + 1) * CW], dw[:, j * P:(j + 1) * P], c.ident[0:CW, 0:CW]).then_inc(turned, 1)
                    pe.transpose(ps[:, 2, j * HIST:(j + 1) * HIST], hist[:, j * P:(j + 1) * P],
                                 c.ident[0:HIST, 0:HIST]).then_inc(turned, 1)

            @block.vector
            def _(dve):
                dve.memset(c.aT[:, :, 0:HIST], 0.0).then_inc(kept, 1)
                dve.memset(c.eps[:], EPS).then_inc(kept, 1)
                dve.wait_ge(turned, S0 + 1 + 2 * CT)
                dve.tensor_copy(c.vec[:], ps[:, 0, 0:V_ROWS]).then_inc(kept, 1)
                dve.tensor_copy(c.dw[:], ps[:, 1, 0:CT * CW].rearrange("p (j k) -> p j k", j=CT)).then_inc(kept, 1)
                dve.tensor_copy(c.aT[:, :, HIST + SEQ:2 * HIST + SEQ],
                                ps[:, 2, 0:CT * HIST].rearrange("p (j k) -> p j k", j=CT)).then_inc(kept, 1)
                dve.wait_ge(kept, S0 + 5)


class Chunk:

    def __init__(self, name, kind, bank, src, width, head=0, gain=None, rows_out=None, turn=None, turned_out=None):
        self.name, self.kind, self.bank, self.src, self.width = name, kind, bank, src, width
        self.head, self.gain, self.rows_out, self.turn, self.turned_out = head, gain, rows_out, turn, turned_out


def project(nc, c, tag, x_tile, vec0, weights, chunks, tiles, xT_out=None, forget=None, a_cols=None):
    with Phase(nc, tag) as p:
        ncols = sum(ch.width for ch in chunks)
        w = p.sb(f"w", [P, KC, ncols])
        col = {}
        at = 0
        for ch in chunks:
            col[ch.name] = at
            at += ch.width
        x = [p.sb(f"x{b}", [P, D]) for b in range(2)]
        xT = [p.sb(f"xT{b}", [P, KC, P]) for b in range(2)]
        junk = p.sb(f"junk", [P, D])
        ssx, rx = p.sb(f"ssx", [P, 1]), p.sb(f"rx", [P, 1])
        norms = [ch for ch in chunks if ch.kind == "norm"]
        turns = [ch for ch in chunks if ch.turn]
        squares = {ch.name: p.sb(f"sq_{ch.name}", [P, BANK]) for ch in norms}
        sums = {ch.name: p.sb(f"ss_{ch.name}", [P, BANK // ch.head]) for ch in norms}
        scales = {ch.name: p.sb(f"rs_{ch.name}", [P, BANK // ch.head]) for ch in norms}
        gains = {ch.name: p.sb(f"gain_{ch.name}", [P, ch.head]) for ch in norms}
        rows = {ch.name: p.sb(f"rows_{ch.name}", [P, BANK]) for ch in chunks if ch.kind != "forget"}
        stage = {ch.name: p.sb(f"turned_{ch.name}", [ch.turn, BANK // ch.turn, P]) for ch in turns if ch.turned_out}
        pT, pC, pX, pY = p.banks(f"pT", 2), p.banks(f"pC", 3), p.banks(f"pX", 2), p.banks(f"pY", 1)
        s_w = {ch.name: p.sem(f"w_{ch.name}_in_sbuf") for ch in chunks}
        s_gain, s_zero = p.sem("gains_in_sbuf"), p.sem("x_pad_zeroed")
        s_x = p.sems("x_in_sbuf", 2)
        s_ssx, s_rx, s_rxi, s_xn = (p.sem(n) for n in ("x_squares", "x_root", "x_scale", "x_normed"))
        s_xturn, s_xT = p.sems("x_turned", 2), p.sem("xT_in_sbuf")
        s_xTout = p.sems("xT_stored", 2)
        s_chunk = p.sems("chunk_done", 2)
        s_free = [p.sem(f"bank{k}_read") for k in range(3)]
        s_open = p.sem("turn_opened")
        s_sq, s_ss, s_rs, s_rsi, s_z1 = (p.sem(f"head_{n}") for n in ("squares", "sums", "roots", "scales", "scaled"))
        s_rows = {ch.name: p.sem(f"{ch.name}_rows_ready") for ch in chunks}
        s_rout = {ch.name: p.sem(f"{ch.name}_rows_stored") for ch in chunks if ch.rows_out}
        s_turn = {ch.name: p.sem(f"{ch.name}_turned") for ch in turns}
        s_keep = {ch.name: p.sem(f"{ch.name}T_in_sbuf") for ch in turns}
        s_tout = {ch.name: p.sem(f"{ch.name}T_stored") for ch in turns if ch.turned_out}
        n_chunks, n_norms = len(chunks), len(norms)
        users = {k: [ch for ch in chunks if ch.bank == k] for k in range(3)}
        x_users = [ch for ch in turns if ch.turn == DF]
        y_users = [ch for ch in turns if ch.turn == P]

        def before(ch):
            line = x_users if ch.turn == DF else y_users
            k = line.index(ch)
            return (line[k - 1], 0) if k else (line[-1], 1)

        def bank_of(ch):
            return (pX[0:DF, :, :].rearrange("p a (h t) -> p (a h) t", t=P) if ch.turn == DF
                    else pY[:, 0, :].rearrange("p (h t) -> p h t", t=P))

        p.start()
        with nc.Block() as block:
            @block.sync
            def _(sp):
                sp.dma_start(x[0][:], x_tile(Tile(0, 0))).then_inc(s_x[0], 16)
                for ch in norms:
                    sp.dma_start(gains[ch.name][:], ch.gain.partition_broadcast(P)).then_inc(s_gain, 16)
                for ch in chunks:
                    sp.dma_start(w[:, :, col[ch.name]:col[ch.name] + ch.width],
                                 weights[:, ch.src:ch.src + ch.width].rearrange("(k p) n -> p k n", p=P))\
                      .then_inc(s_w[ch.name], 16)

                def load(T):
                    n = SAM if T.sample else P
                    sp.wait_ge(s_xturn[T.b], S0 + T.u)
                    sp.dma_start(x[T.b][0:n, :], x_tile(T)).then_inc(s_x[T.b], 16)

                def emit(T):
                    n = SAM if T.sample else P
                    if not T.last:
                        load(T.next())
                    if xT_out is not None:
                        sp.wait_ge(s_xT, S0 + T.n + 1)
                        sp.dma_start(xT_out(T), xT[T.b][:].rearrange("p k t -> p (k t)")).then_inc(s_xTout[T.b], 16)
                    for ch in chunks:
                        if ch.rows_out:
                            sp.wait_ge(s_rows[ch.name], S0 + T.n + 1)
                            sp.dma_start(ch.rows_out(T), rows[ch.name][0:n, :]).then_inc(s_rout[ch.name], 16)
                    for ch in turns:
                        if ch.turned_out:
                            sp.wait_ge(s_keep[ch.name], S0 + T.n + 1)
                            sp.dma_start(ch.turned_out(T), stage[ch.name][:]).then_inc(s_tout[ch.name], 16)

                tiles(sp, emit)
                if xT_out is not None:
                    sp.wait_ge(s_xTout[0], S0 + 16 * ((tiles.count + 1) // 2))
                    sp.wait_ge(s_xTout[1], S0 + 16 * (tiles.count // 2))
                for s in list(s_rout.values()) + list(s_tout.values()):
                    sp.wait_ge(s, S0 + 16 * tiles.count)

            @block.scalar
            def _(act):
                def square(T):
                    act.wait_ge(s_x[T.b], S0 + 16 * (T.u + 1))
                    if T.sample:
                        act.wait_ge(s_zero, S0 + 1)
                    act.wait_ge(s_rx, S0 + T.n)
                    act.wait_ge(s_ssx, S0 + T.n)
                    act.activation(junk[:], x[T.b][:], ACT.Square, accum_out=ssx[:]).then_inc(s_ssx, 1)
                    act.wait_ge(s_ssx, S0 + T.n + 1)
                    act.wait_ge(s_xn, S0 + T.n)
                    act.activation(rx[:], ssx[:], ACT.Sqrt, scale=1.0 / D, bias=c.eps[:, 0:1]).then_inc(s_rx, 1)

                def keep_xT(T):
                    act.wait_ge(s_xturn[T.b], S0 + T.u + 1)
                    if xT_out is not None:
                        act.wait_ge(s_xTout[T.b], S0 + 16 * T.u)
                    act.wait_ge(s_chunk[T.b], S0 + n_chunks * T.u)
                    for k in range(KC):
                        ins = act.activation(xT[T.b][:, k, :], pT[:, k // 4, (k % 4) * P:(k % 4 + 1) * P], ACT.Copy,
                                             scale=c.vec[:, vec0 + k:vec0 + k + 1])
                    ins.then_inc(s_xT, 1)

                def emit(T):
                    if not T.last:
                        square(T.next())
                    for k, ch in enumerate(chunks):
                        if ch.kind == "norm":
                            act.wait_ge(s_chunk[T.b], S0 + n_chunks * T.u + k + 1)
                            act.wait_ge(s_ss, S0 + n_norms * T.n + norms.index(ch))
                            act.activation(squares[ch.name][:], pC[:, ch.bank, :], ACT.Square).then_inc(s_sq, 1)
                            act.wait_ge(s_ss, S0 + n_norms * T.n + norms.index(ch) + 1)
                            act.wait_ge(s_z1, S0 + n_norms * T.n + norms.index(ch))
                            act.activation(scales[ch.name][:], sums[ch.name][:], ACT.Sqrt, scale=1.0 / ch.head,
                                           bias=c.eps[:, 0:1]).then_inc(s_rs, 1)
                        if ch.kind == "glu_gate":
                            act.wait_ge(s_chunk[T.b], S0 + n_chunks * T.u + k + 1)
                            act.wait_ge(s_rows["ga"], S0 + T.n)
                            act.activation(rows[ch.name][:], pC[:, ch.bank, :], ACT.Sigmoid).then_inc(s_rows[ch.name], 1)
                    if not T.last:
                        keep_xT(T.next())
                    for ch in turns:
                        act.wait_ge(s_turn[ch.name], S0 + T.n + 1)
                        if ch.turned_out:
                            act.wait_ge(s_tout[ch.name], S0 + 16 * T.n)
                            act.activation(stage[ch.name][:], bank_of(ch), ACT.Copy).then_inc(s_keep[ch.name], 1)
                        else:
                            n = SAM if T.sample else P
                            act.activation(a_cols(T), bank_of(ch)[:, :, 0:n], ACT.Copy).then_inc(s_keep[ch.name], 1)
                square(Tile(0, 0))
                keep_xT(Tile(0, 0))
                tiles(act, emit)

            @block.tensor
            def _(pe):
                def turn_x(T):
                    pe.wait_ge(s_xn, S0 + T.n + 1)
                    pe.wait_ge(s_xT, S0 + T.n)
                    for k in range(KC):
                        ins = pe.transpose(pT[:, k // 4, (k % 4) * P:(k % 4 + 1) * P], x[T.b][:, k * P:(k + 1) * P], c.ident[:])
                    ins.then_inc(s_xturn[T.b], 1)

                def emit(T):
                    pe.wait_ge(s_xT, S0 + T.n + 1)
                    for ch in chunks:
                        if isinstance(T.u, int) or T.b == 0:
                            pe.wait_ge(s_w[ch.name], S0 + 16)
                        line = users[ch.bank]
                        pe.wait_ge(s_free[ch.bank], S0 + len(line) * T.n + line.index(ch))
                        for k in range(KC):
                            ins = pe.matmul(pC[:, ch.bank, 0:ch.width], xT[T.b][:, k, :],
                                            w[:, k, col[ch.name]:col[ch.name] + ch.width], start=(k == 0), stop=(k == KC - 1))
                        ins.then_inc(s_chunk[T.b], 1)
                    if not T.last:
                        turn_x(T.next())
                    for ch in turns:
                        pe.wait_ge(s_rows[ch.name], S0 + T.n + 1)
                        prev, back = before(ch)
                        pe.wait_ge(s_keep[prev.name], S0 + T.n + 1 - back)
                        pe.sem_inc(s_open, 1)
                        for h in range(BANK // ch.turn):
                            ins = pe.transpose(bank_of(ch)[:, h, :], rows[ch.name][:, h * ch.turn:(h + 1) * ch.turn], c.ident[:])
                        ins.then_inc(s_turn[ch.name], 1)
                turn_x(Tile(0, 0))
                tiles(pe, emit)

            @block.vector
            def _(dve):
                def norm_x(T):
                    dve.wait_ge(s_rx, S0 + T.n + 1)
                    dve.wait_ge(s_x[T.b], S0 + 16 * (T.u + 1))
                    dve.reciprocal(rx[:], rx[:]).then_inc(s_rxi, 1)
                    dve.wait_ge(s_rxi, S0 + T.n + 1)
                    dve.tensor_scalar(x[T.b][:], x[T.b][:], rx[:, 0:1], None, ALU.mult).then_inc(s_xn, 1)

                def emit(T):
                    n = T.n
                    if not T.last:
                        N = T.next()
                        if N.sample:
                            dve.wait_ge(s_xturn[N.b], S0 + N.u)
                            dve.memset(x[N.b][SAM:P, :], 0.0).then_inc(s_zero, 1)
                            dve.wait_ge(s_zero, S0 + 1)
                        norm_x(N)
                    for k, ch in enumerate(chunks):
                        if ch.kind == "norm":
                            m = norms.index(ch)
                            H = BANK // ch.head
                            heads = lambda ap: ap.rearrange("p (h d) -> p h d", d=ch.head)
                            dve.wait_ge(s_sq, S0 + n_norms * n + m + 1)
                            dve.wait_ge(s_rs, S0 + n_norms * n + m)
                            dve.tensor_reduce(sums[ch.name][:], heads(squares[ch.name][:]), AX, ALU.add).then_inc(s_ss, 1)
                            dve.wait_ge(s_rs, S0 + n_norms * n + m + 1)
                            dve.reciprocal(scales[ch.name][:], scales[ch.name][:]).then_inc(s_rsi, 1)
                            dve.wait_ge(s_rsi, S0 + n_norms * n + m + 1)
                            if ch.turn:
                                dve.wait_ge(s_turn[ch.name], S0 + n)
                            if ch.rows_out:
                                dve.wait_ge(s_rout[ch.name], S0 + 16 * n)
                            dve.tensor_tensor(heads(rows[ch.name][:]), heads(pC[:, ch.bank, :]),
                                              scales[ch.name][:].unsqueeze(2).broadcast_to([P, H, ch.head]), ALU.mult)\
                               .then_inc(s_z1, 1)
                            dve.wait_ge(s_z1, S0 + n_norms * n + m + 1)
                            dve.sem_inc(s_free[ch.bank], 1)
                            dve.tensor_tensor(heads(rows[ch.name][:]), heads(rows[ch.name][:]),
                                              gains[ch.name][:].unsqueeze(1).broadcast_to([P, H, ch.head]),
                                              ALU.mult).then_inc(s_rows[ch.name], 1)
                        elif ch.kind == "copy":
                            dve.wait_ge(s_chunk[T.b], S0 + n_chunks * T.u + k + 1)
                            dve.wait_ge(s_rout[ch.name], S0 + 16 * n)
                            dve.tensor_copy(rows[ch.name][:], pC[:, ch.bank, :]).then_inc(s_rows[ch.name], 1)
                            dve.wait_ge(s_rows[ch.name], S0 + n + 1)
                            dve.sem_inc(s_free[ch.bank], 1)
                        elif ch.kind == "glu_gate":
                            a = next(o for o in chunks if o.name == "ga")
                            dve.wait_ge(s_rows[ch.name], S0 + n + 1)
                            dve.wait_ge(s_rout["ga"], S0 + 16 * n)
                            dve.wait_ge(s_turn["ga"], S0 + n)
                            dve.tensor_tensor(rows["ga"][:], pC[:, a.bank, :], rows[ch.name][:], ALU.mult).then_inc(s_rows["ga"], 1)
                            dve.wait_ge(s_rows["ga"], S0 + n + 1)
                            dve.sem_inc(s_free[a.bank], 1)
                            dve.sem_inc(s_free[ch.bank], 1)
                        elif ch.kind == "forget":
                            dve.wait_ge(s_chunk[T.b], S0 + n_chunks * T.u + k + 1)
                            dve.tensor_copy(forget[:, T.n, :], pC[:, ch.bank, 0:ch.width]).then_inc(s_rows[ch.name], 1)
                            dve.wait_ge(s_rows[ch.name], S0 + n + 1)
                            dve.sem_inc(s_free[ch.bank], 1)
                dve.wait_ge(s_gain, S0 + 16 * n_norms)
                norm_x(Tile(0, 0))
                tiles(dve, emit)


def decay(nc, io, scr, c):
    NC = PAST // P
    with Phase(nc, "decay") as p:
        bias = p.sb("forget_bias", [P, HF])
        t, e, l, logf = (p.sb(n, [P, NT + 1, HF]) for n in ("decay_t", "decay_e", "decay_l", "decay_logf"))
        lT = p.sb("logf_T", [HF, TOK])
        cum = p.sb("cum_T", [HF, TOK])
        zeros = p.sb("scan_zeros", [HF, TOK])
        ones_row = p.sb("ones_row", [HF, PAST + TOK])
        past = p.sb("past_logf", [P, NC, HF])
        past_T = p.sb("past_T", [HF, PAST])
        suffix = p.sb("suffix_T", [HF, PAST])
        key_row = p.sb("key_row", [HF, PAST + TOK])
        query_row = p.sb("query_row", [HF, TOK])
        ck = p.sb("cached_k", [P, NC, HF * DF])
        ckT = p.sb("cached_kT", [DF, 2, HF, P])
        cm = p.sb("cached_mk", [P, NMEM // P, HM * DM])
        cmT = p.sb("cached_mkT", [P, 2, HM, P])
        pL = p.banks("p_logf", 3)
        pP = p.banks("p_past", 1)
        pK = p.banks("p_keys", 4)
        loaded, stored, key_stored = p.sem("d_loaded"), p.sem("d_stored"), p.sems("cached_keys_stored", 2)
        abs_, exp_, log_, done = (p.sem(n) for n in ("d_abs", "d_exp", "d_log", "d_logf"))
        turned, past_turned, pkeys, kept = (p.sem(n) for n in ("d_turned", "d_past_turned", "d_keys_turned", "d_keys_kept"))
        v, rows_ready = p.sem("d_vector_step"), p.sem("d_rows_ready")
        p.start()
        with nc.Block() as block:
            @block.sync
            def _(sp):
                sp.dma_start(bias[:], io["b_forget"][0].partition_broadcast(P)).then_inc(loaded, 16)
                sp.dma_start(past[:], io["cache_fox_logf"][0, 0].rearrange("(t p) h -> p t h", p=P)).then_inc(loaded, 16)
                sp.dma_start(ck[:], io["cache_fox_k"][0, 0].rearrange("(t p) h d -> p t (h d)", p=P)).then_inc(loaded, 16)
                sp.dma_start(cm[:], io["cache_mem_k"][0, 0].rearrange("(t p) h d -> p t (h d)", p=P)).then_inc(loaded, 16)
                for i in range(NC):
                    sp.wait_ge(kept, S0 + i + 1)
                    sp.dma_start(scr["kT"][:, 0:DF, SEQ + i * P:SEQ + (i + 1) * P].rearrange("h d t -> d h t"),
                                 ckT[:, i % 2, :, :]).then_inc(key_stored[i % 2], 16)
                for i in range(NMEM // P):
                    sp.wait_ge(kept, S0 + NC + i + 1)
                    sp.dma_start(scr["mkT"][1, :, :, i * P:(i + 1) * P].rearrange("h d t -> d h t"),
                                 cmT[:, i % 2, :, :]).then_inc(stored, 16)
                sp.wait_ge(done, S0 + 1)
                sp.dma_start(io["fox_logf_prompt"][0, 0].rearrange("(t p) h -> p t h", p=P), logf[:, 0:NT, :]).then_inc(stored, 16)
                sp.dma_start(io["fox_logf_sample"][0, 0], logf[0:SAM, NT, :]).then_inc(stored, 16)
                sp.wait_ge(rows_ready, S0 + 1)
                sp.dma_start(scr["kT"][:, DF, :], key_row[:]).then_inc(stored, 16)
                sp.dma_start(scr["kT"][:, DF + 1, :], ones_row[:]).then_inc(stored, 16)
                sp.dma_start(scr["qT"][:, DF, :], ones_row[:, 0:TOK]).then_inc(stored, 16)
                sp.dma_start(scr["qT"][:, DF + 1, :], query_row[:]).then_inc(stored, 16)
                sp.dma_start(io["conv_prompt"][0, 0], scr["a"][SEQ - HIST:SEQ, :]).then_inc(stored, 16)
                sp.dma_start(io["conv_sample"][0, 0], scr["a"][SEQ + SAM - HIST:SEQ + SAM, :]).then_inc(stored, 16)
                sp.wait_ge(stored, S0 + 16 * (NMEM // P + 8))
                for b in range(2):
                    sp.wait_ge(key_stored[b], S0 + 16 * NC // 2)

            @block.scalar
            def _(act):
                act.wait_ge(abs_, S0 + 1)
                act.activation(e[:], e[:], ACT.Exp, scale=-1.0).then_inc(exp_, 1)
                act.wait_ge(exp_, S0 + 1)
                act.activation(l[:], e[:], ACT.Ln, bias=1.0).then_inc(log_, 1)
                for i in range(NC):
                    act.wait_ge(pkeys, S0 + i + 1)
                    if i >= 2:
                        act.wait_ge(key_stored[i % 2], S0 + 16 * (i // 2))
                    act.activation(ckT[:, i % 2, :, :], pK[0:DF, 2 * (i % 2):2 * (i % 2) + 2, :].rearrange("p a (h t) -> p (a h) t", t=P),
                                   ACT.Copy).then_inc(kept, 1)
                for i in range(NMEM // P):
                    act.wait_ge(pkeys, S0 + NC + i + 1)
                    act.activation(cmT[:, i % 2, :, :], pK[:, 2 * (i % 2), :].rearrange("p (h t) -> p h t", t=P),
                                   ACT.Copy).then_inc(kept, 1)

            @block.tensor
            def _(pe):
                pe.wait_ge(loaded, S0 + 64)
                for i in range(NC):
                    ins = pe.transpose(pP[0:HF, 0, i * P:(i + 1) * P], past[:, i, :], c.ident[:])
                ins.then_inc(past_turned, 1)
                for i in range(NC):
                    if i >= 2:
                        pe.wait_ge(kept, S0 + i - 1)
                    for h in range(HF):
                        ins = pe.transpose(pK[0:DF, 2 * (i % 2) + h // 4, (h % 4) * P:(h % 4 + 1) * P],
                                           ck[:, i, h * DF:(h + 1) * DF], c.ident[:])
                    ins.then_inc(pkeys, 1)
                for i in range(NMEM // P):
                    pe.wait_ge(kept, S0 + NC + i - 1)
                    for h in range(HM):
                        ins = pe.transpose(pK[:, 2 * (i % 2), h * P:(h + 1) * P], cm[:, i, h * P:(h + 1) * P], c.ident[:])
                    ins.then_inc(pkeys, 1)
                pe.wait_ge(done, S0 + 1)
                for i in range(NT + 1):
                    ins = pe.transpose(pL[0:HF, i // 4, (i % 4) * P:(i % 4 + 1) * P], logf[:, i, :], c.ident[:])
                ins.then_inc(turned, 1)

            @block.vector
            def _(dve):
                s = Chain(dve, v)
                s.step(dve.memset(zeros[:], 0.0))
                s.step(dve.memset(ones_row[:], 1.0))
                dve.wait_ge(loaded, S0 + 64)
                s.link(dve.tensor_tensor(t[:], c.forget[:], bias[:].unsqueeze(1).broadcast_to([P, NT + 1, HF]), ALU.add))
                s.link(dve.tensor_scalar(e[:], t[:], -1.0, None, ALU.mult))
                dve.tensor_tensor(e[:], e[:], t[:], ALU.max).then_inc(abs_, 1)
                dve.wait_ge(log_, S0 + 1)
                dve.scalar_tensor_tensor(logf[:], t[:], 0.0, l[:], ALU.min, ALU.subtract).then_inc(done, 1)
                dve.wait_ge(past_turned, S0 + 1)
                s.link(dve.tensor_copy(past_T[:], pP[0:HF, 0, :][:, ::-1]))
                s.link(dve.tensor_tensor_scan(suffix[:], past_T[:], zeros[:, 0:PAST], 0.0, ALU.add, ALU.add))
                s.link(dve.tensor_tensor(suffix[:], suffix[:], past_T[:], ALU.subtract))
                s.link(dve.tensor_scalar(key_row[:, SEQ:SEQ + PAST], suffix[:, ::-1], float(DF) ** 0.5, None, ALU.mult))
                dve.wait_ge(turned, S0 + 1)
                s.link(dve.tensor_copy(lT[:, 0:SEQ], pL[0:HF, 0:2, :].rearrange("p a t -> p (a t)")))
                s.link(dve.tensor_copy(lT[:, SEQ:TOK], pL[0:HF, 2, 0:P]))
                s.link(dve.tensor_tensor_scan(cum[:, 0:SEQ], lT[:, 0:SEQ], zeros[:, 0:SEQ], 0.0, ALU.add, ALU.add))
                s.link(dve.tensor_tensor_scan(cum[:, SEQ:TOK], lT[:, SEQ:TOK], zeros[:, SEQ:TOK], 0.0, ALU.add, ALU.add))
                s.link(dve.tensor_scalar(query_row[:], cum[:], float(DF) ** 0.5, None, ALU.mult))
                s.link(dve.tensor_scalar(key_row[:, 0:SEQ], cum[:, 0:SEQ], -float(DF) ** 0.5, None, ALU.mult))
                dve.tensor_scalar(key_row[:, SEQ + PAST:], cum[:, SEQ:TOK], -float(DF) ** 0.5, None, ALU.mult).then_inc(rows_ready, 1)


def gates_and_conv(nc, io, scr, c):
    NG = GATES // BANK
    with Phase(nc, "gates") as p:
        w = p.sb("w_gates", [P, KC, GATES])
        xT = [p.sb(f"gate_xT{b}", [P, KC, P]) for b in range(2)]
        g = p.sb("gate_rows", [P, 3, 2 * BANK])
        y = [p.sb(f"conv_y{b}", [P, CONV_OUT]) for b in range(CT)]
        ps = p.banks("p_gates", 6)
        s_w = p.sems("gate_w_in_sbuf", NG)
        s_x = p.sems("gate_xT_in_sbuf", 2)
        s_chunk, s_sig = p.sems("gate_product", 2), p.sem("gate_sigmoid")
        s_out = p.sems("gates_stored", 3)
        tap, y_done, y_out = p.sem("conv_tap"), p.sem("conv_done"), p.sem("conv_stored")
        p.start()
        with nc.Block() as block:
            @block.sync
            def _(sp):
                sp.dma_start(xT[0][:].rearrange("p k t -> p (k t)"), scr["xT"][0]).then_inc(s_x[0], 16)
                for k in range(NG):
                    sp.dma_start(w[:, :, k * BANK:(k + 1) * BANK],
                                 io["w_in"][0, :, C_G + k * BANK:C_G + (k + 1) * BANK].rearrange("(k p) n -> p k n", p=P))\
                      .then_inc(s_w[k], 16)

                def load(T):
                    sp.wait_ge(s_chunk[T.b], S0 + NG * T.u)
                    sp.dma_start(xT[T.b][:].rearrange("p k t -> p (k t)"), scr["xT"][T.n]).then_inc(s_x[T.b], 16)

                def emit(T):
                    if not T.last:
                        load(T.next())
                    for k in range(3):
                        sp.wait_ge(s_sig, S0 + NG + NG * T.n + 2 * k + 2)
                        sp.dma_start(scr["gates"][T.n, :, 2 * k * BANK:2 * (k + 1) * BANK], g[:, k, :]).then_inc(s_out[k], 16)
                all_tiles(sp, emit)
                for j in range(CT):
                    sp.wait_ge(y_done, S0 + j + 1)
                    sp.dma_start(scr["y"][j], y[j][:]).then_inc(y_out, 16)
                sp.wait_ge(y_out, S0 + 16 * CT)
                for k in range(3):
                    sp.wait_ge(s_out[k], S0 + 16 * (NT + 1))

            @block.tensor
            def _(pe):
                for k in range(NG):
                    pe.wait_ge(s_w[k], S0 + 16)

                def emit(T):
                    pe.wait_ge(s_x[T.b], S0 + 16 * (T.u + 1))
                    for j in range(NG):
                        pe.wait_ge(s_sig, S0 + NG * T.n + j + 1)
                        for k in range(KC):
                            ins = pe.matmul(ps[:, j, :], xT[T.b][:, k, :], w[:, k, j * BANK:(j + 1) * BANK],
                                            start=(k == 0), stop=(k == KC - 1))
                        ins.then_inc(s_chunk[T.b], 1)
                all_tiles(pe, emit)

            @block.scalar
            def _(act):
                act.sem_inc(s_sig, NG)

                def emit(T):
                    for j in range(NG):
                        act.wait_ge(s_chunk[T.b], S0 + NG * T.u + j + 1)
                        act.wait_ge(s_out[j // 2], S0 + 16 * T.n)
                        act.activation(g[:, j // 2, (j % 2) * BANK:(j % 2 + 1) * BANK], ps[:, j, :], ACT.Sigmoid).then_inc(s_sig, 1)
                all_tiles(act, emit)

            @block.vector
            def _(dve):
                s = Chain(dve, tap)
                for j in range(CT):
                    a, yj = c.aT[:, j, :], y[j]
                    s.link(dve.tensor_scalar(yj[:], a[:, 0:CONV_OUT], c.dw[:, j, 0:1], c.vec[:, V_BDW + j:V_BDW + j + 1],
                                             ALU.mult, ALU.add))
                    for k in range(1, CW):
                        ins = dve.scalar_tensor_tensor(yj[:], a[:, k:k + CONV_OUT], c.dw[:, j, k:k + 1], yj[:], ALU.mult, ALU.add)
                        if k == CW - 1:
                            ins.then_inc(y_done, 1)
                        else:
                            s.link(ins)


class Unit:

    def __init__(self, q_at, rows, k_at, keys, values, masked, out_tile):
        self.q_at, self.rows, self.k_at, self.keys = q_at, rows, k_at, keys
        self.values, self.masked, self.out_tile = values, masked, out_tile
        self.groups = [values[i:i + 4] for i in range(0, len(values), 4)]


SLOTS = 3


def attention(nc, c, tag, heads, K, dh, q_cols, k_cols, v_tiles, units, loads, out):
    scale = float(dh) ** -0.5
    U = len(units)
    n_groups = sum(len(u.groups) for u in units)
    assert 2 * U % SLOTS == 0 and max(len(u.groups) for u in units) <= 2
    with Phase(nc, tag) as p:
        qT = [p.sb(f"qT{b}", [K, q_cols]) for b in range(2)]
        kT = [p.sb(f"kT{b}", [K, k_cols]) for b in range(2)]
        v = [p.sb(f"v{b}", [P, v_tiles, dh]) for b in range(2)]
        probs = [p.sb(f"probs{b}", [P, 2 * BANK]) for b in range(SLOTS)]
        pT = [p.sb(f"probs_T{b}", [P, 8, P]) for b in range(SLOTS)]
        o = [p.sb(f"o{b}", [P, dh]) for b in range(SLOTS)]
        top, bias, total, inv = (p.sb(n, [P, SLOTS]) for n in ("row_max", "exp_bias", "row_sum", "row_scale"))
        S = [p.banks(f"scores{b}", 2) for b in range(SLOTS)]
        T = p.banks("turned", 1)
        O = p.banks("out", 1)
        s_in, s_head = p.sems("head_in_sbuf", 2), p.sems("head_done", 2)
        s_scores, s_max, s_bias, s_exp = (p.sems(n, SLOTS) for n in ("scored", "max", "bias", "exp"))
        s_turn, s_kept = p.sems("probs_turned", 2), p.sems("probs_T_kept", 2)
        s_pv, s_inv, s_o, s_out = (p.sems(n, SLOTS) for n in ("pv", "scale", "o", "o_stored"))
        s_open = p.sem("sample_opened")
        n_loads = len(loads(0, 0))

        class At:
            def __init__(self, i, b, m):
                w = b * U + m
                self.b, self.m, self.unit, self.slot, self.before = b, m, units[m], w % SLOTS, 2 * U // SLOTS * i + w // SLOTS
                g = b * n_groups + sum(len(u.groups) for u in units[:m])
                self.group = [((g + k) % 2, n_groups * i + (g + k) // 2) for k in range(len(self.unit.groups))]
                self.last_slot, self.last_use = (w - 1) % SLOTS, 2 * U // SLOTS * i + (w + SLOTS - 1) // SLOTS
                self.former = [((g + k - 1) % 2, n_groups * i + (g + k + 1) // 2) for k in range(len(self.unit.groups))]

        def line(i):
            return [At(i, b, m) for b in range(2) for m in range(U)]

        def turns(eng, first, rest):
            with eng.Fori(0, heads // 2) as i:
                units_of = line(i)
                for a in units_of[:2]:
                    first(i, a)
                for k, a in enumerate(units_of):
                    rest(i, a, units_of[k + 2] if k + 2 < len(units_of) else None)

        p.start()
        with nc.Block() as block:
            @block.tensor
            def _(pe):
                def score_bank(i, a, k):
                    u = a.unit
                    if k >= u.keys:
                        return
                    if k == 0:
                        if a.m == 0:
                            pe.wait_ge(s_in[a.b], S0 + 16 * n_loads * (i + 1))
                        pe.wait_ge(s_exp[a.slot], S0 + a.before)
                    n = min(BANK, u.keys - k)
                    last = k + n == u.keys
                    ins = pe.matmul(S[a.slot][0:u.rows, k // BANK, 0:n], qT[a.b][:, u.q_at:u.q_at + u.rows],
                                    kT[a.b][:, u.k_at + k:u.k_at + k + n], start=True, stop=not (last and u.masked))
                    if last and u.masked:
                        ins = pe.matmul(S[a.slot][0:u.rows, k // BANK, n - u.rows:n], c.ident[:, 0:u.rows],
                                        c.causal[:, 0:u.rows], start=False, stop=True)
                    if last:
                        ins.then_inc(s_scores[a.slot], 1)

                def scores(i, a):
                    for k in range(2):
                        score_bank(i, a, k * BANK)

                def rest(i, a, ahead):
                    u = a.unit
                    pe.wait_ge(s_exp[a.slot], S0 + a.before + 1)
                    for k in range(2):
                        if k < len(u.groups):
                            g, former, kept = a.group[k][0], *a.former[k]
                            pe.wait_ge(s_kept[former], S0 + kept)
                            if u.rows < P:
                                pe.sem_inc(s_open, 1)
                            for n, (vt, keys) in enumerate(u.groups[k]):
                                at = (vt - u.values[0][0]) * P
                                ins = pe.transpose(T[0:keys, 0, n * P:n * P + u.rows], probs[a.slot][0:u.rows, at:at + keys],
                                                   c.ident[0:u.rows, 0:u.rows])
                            ins.then_inc(s_turn[g], 1)
                        if ahead is not None:
                            score_bank(i, ahead, k * BANK)
                    pe.wait_ge(s_o[a.last_slot], S0 + a.last_use)
                    for (g, used), tiles in zip(a.group, u.groups):
                        pe.wait_ge(s_kept[g], S0 + used + 1)
                        if u.rows < P:
                            pe.sem_inc(s_open, 1)
                        for vt, keys in tiles:
                            k = vt - u.values[0][0]
                            ins = pe.matmul(O[0:u.rows, 0, a.slot * dh:(a.slot + 1) * dh], pT[a.slot][0:keys, k, 0:u.rows],
                                            v[a.b][0:keys, vt, :], start=(k == 0), stop=(k == len(u.values) - 1))
                    ins.then_inc(s_pv[a.slot], 1)
                    if a.m == U - 1:
                        pe.wait_ge(s_pv[a.slot], S0 + a.before + 1)
                        pe.sem_inc(s_head[a.b], 1)
                turns(pe, scores, rest)

            def keep(eng, copy, a, g_slot):
                u = a.unit
                for (g, used), tiles in zip(a.group, u.groups):
                    if g != g_slot:
                        continue
                    eng.wait_ge(s_turn[g], S0 + used + 1)
                    eng.wait_ge(s_pv[a.slot], S0 + a.before)
                    full = [t for t in tiles if t[1] == P]
                    k0 = tiles[0][0] - u.values[0][0]
                    ins = None
                    if full:
                        ins = copy(pT[a.slot][:, k0:k0 + len(full), 0:u.rows],
                                   T[:, 0, 0:len(full) * P].rearrange("p (k t) -> p k t", t=P)[:, :, 0:u.rows])
                    if len(full) < len(tiles):
                        n = tiles[-1][1]
                        k = len(full)
                        ins = copy(pT[a.slot][0:n, k0 + k, 0:u.rows], T[0:n, 0, k * P:k * P + u.rows])
                    ins.then_inc(s_kept[g], 1)

            @block.scalar
            def _(act):
                def exps(i, a):
                    u, s = a.unit, a.slot
                    act.wait_ge(s_bias[s], S0 + a.before + 1)
                    act.wait_ge(s_pv[s], S0 + a.before)
                    act.wait_ge(s_inv[s], S0 + a.before)
                    act.activation(probs[s][0:u.rows, 0:u.keys],
                                   S[s][0:u.rows, :, :].rearrange("p a n -> p (a n)")[:, 0:u.keys], ACT.Exp,
                                   bias=bias[0:u.rows, s:s + 1], scale=scale, accum_out=total[0:u.rows, s:s + 1]).then_inc(s_exp[s], 1)

                def rest(i, a, ahead):
                    keep(act, lambda dst, src: act.activation(dst, src, ACT.Copy), a, 0)
                    if ahead is not None:
                        exps(i, ahead)
                turns(act, exps, rest)

            @block.vector
            def _(dve):
                def maxes(i, a):
                    u, s = a.unit, a.slot
                    dve.wait_ge(s_scores[s], S0 + a.before + 1)
                    dve.tensor_reduce(top[0:u.rows, s:s + 1], S[s][0:u.rows, :, :].rearrange("p a n -> p (a n)")[:, 0:u.keys],
                                      AX, ALU.max).then_inc(s_max[s], 1)
                    dve.wait_ge(s_max[s], S0 + a.before + 1)
                    dve.wait_ge(s_exp[s], S0 + a.before)
                    dve.tensor_scalar(bias[0:u.rows, s:s + 1], top[0:u.rows, s:s + 1], -scale, None, ALU.mult).then_inc(s_bias[s], 1)

                def rest(i, a, ahead):
                    u, s = a.unit, a.slot
                    keep(dve, lambda dst, src: dve.tensor_copy(dst, src), a, 1)
                    if ahead is not None:
                        maxes(i, ahead)
                    dve.wait_ge(s_exp[s], S0 + a.before + 1)
                    dve.wait_ge(s_o[s], S0 + a.before)
                    dve.reciprocal(inv[0:u.rows, s:s + 1], total[0:u.rows, s:s + 1]).then_inc(s_inv[s], 1)
                    dve.wait_ge(s_inv[s], S0 + a.before + 1)
                    dve.wait_ge(s_pv[s], S0 + a.before + 1)
                    dve.wait_ge(s_out[s], S0 + 16 * a.before)
                    dve.tensor_scalar(o[s][0:u.rows, :], O[0:u.rows, 0, s * dh:(s + 1) * dh], inv[0:u.rows, s:s + 1], None, ALU.mult)\
                       .then_inc(s_o[s], 1)
                turns(dve, maxes, rest)

            @block.sync
            def _(sp):
                def store(i, a):
                    sp.wait_ge(s_o[a.slot], S0 + a.before + 1)
                    sp.dma_start(out[a.unit.out_tile, 0:a.unit.rows, bass.ts(2 * i + a.b, dh)], o[a.slot][0:a.unit.rows, :])\
                      .then_inc(s_out[a.slot], 16)
                def load(head, b):
                    for dst, src in loads(head, b):
                        buf = {"qT": qT, "kT": kT, "v": v}[dst[0]][b]
                        sp.dma_start(buf[dst[1:]] if len(dst) > 1 else buf[:], src).then_inc(s_in[b], 16)

                for b in range(2):
                    load(b, b)
                with sp.Fori(0, heads // 2 - 1) as i:
                    for a in line(i):
                        store(i, a)
                        if a.m == U - 1:
                            sp.wait_ge(s_head[a.b], S0 + i + 1)
                            load(2 * i + 2 + a.b, a.b)
                i = heads // 2 - 1
                for a in line(i):
                    store(i, a)
                for s in range(SLOTS):
                    sp.wait_ge(s_out[s], S0 + 16 * (2 * U // SLOTS) * (heads // 2))


def forgetting_attention(nc, io, scr, c):
    n_past = PAST // P
    units = [Unit(t * P, P, 0, (t + 1) * P, [(j, P) for j in range(t + 1)], True, t) for t in range(NT)]
    units.append(Unit(SEQ, SAM, SEQ, PAST + SAM, [(NT + j, P) for j in range(n_past)] + [(NT + n_past, SAM)], True, SAMPLE))
    v_p = io["fox_v_prompt"][0, 0].rearrange("(t p) h d -> h p t d", p=P)
    v_c = io["cache_fox_v"][0, 0].rearrange("(t p) h d -> h p t d", p=P)
    v_s = io["fox_v_sample"][0, 0].rearrange("t h d -> h t d")
    every = slice(None)
    attention(nc, c, "fox", HF, DF + 2, DF, SEQ + SAM, SEQ + PAST + SAM, NT + n_past + 1, units, lambda h, b: [
        (("qT",), scr["qT"][h, :, 0:SEQ + SAM]), (("kT",), scr["kT"][h, :, 0:SEQ + PAST + SAM]),
        (("v", every, slice(0, NT)), v_p[h]), (("v", every, slice(NT, NT + n_past)), v_c[h]),
        (("v", slice(0, SAM), NT + n_past), v_s[h])], scr["fox"])


def memory_attention(nc, io, scr, c):
    M = NMEM // P
    units = [Unit(t * P, P, 0, NMEM, [(j, P) for j in range(M)], False, t) for t in range(NT)]
    units.append(Unit(SEQ, SAM, NMEM, NMEM, [(M + j, P) for j in range(M)], False, SAMPLE))
    v_p = io["mem_v_prompt"][0, 0].rearrange("(t p) h d -> h p t d", p=P)
    v_c = io["cache_mem_v"][0, 0].rearrange("(t p) h d -> h p t d", p=P)
    every = slice(None)
    attention(nc, c, "mem", HM, DM, DM, SEQ + SAM, 2 * NMEM, 2 * M, units, lambda h, b: [
        (("qT",), scr["mqT"][h, :, 0:SEQ + SAM]), (("kT", every, slice(0, NMEM)), scr["mkT"][0, h]),
        (("kT", every, slice(NMEM, 2 * NMEM)), scr["mkT"][1, h]),
        (("v", every, slice(0, M)), v_p[h]), (("v", every, slice(M, 2 * M)), v_c[h])], scr["mem"])


def merge(nc, io, scr, c):
    BK = DC // P
    with Phase(nc, "merge") as p:
        w = {n: p.sb(n, [P, BK, D]) for n in ("w_fox_o", "w_mem_o", "w_conv_o")}
        w_out = p.sb("w_out", [P, KC, D])
        gain = p.sb("norm2_gain", [P, D])
        fox, mem, y, gates, x = ([p.sb(f"{n}{b}", shape) for b in range(2)] for n, shape in (
            ("fox", [P, DC]), ("mem", [P, DC]), ("y", [P, CT, P]), ("gates", [P, GATES]), ("x", [P, D])))
        stats, mv, std, rstd = p.sb("ln_stats", [P, 6]), p.sb("ln_mean_var", [P, 2]), p.sb("ln_std", [P, 1]), p.sb("ln_scale", [P, 1])
        yn = p.sb("y_normed", [P, DC])
        turned = {n: p.sb(f"{n}_T", [P, BK, P]) for n in ("fox", "mem", "conv")}
        m, part = p.sb("merged", [P, D]), p.sb("gated_part", [P, D])
        mT = p.sb("merged_T", [P, KC, P])
        x2, h2, junk = p.sb("x2", [P, D]), p.sb("h2", [P, D]), p.sb("junk", [P, D])
        ss, root, inv = p.sb("x2_sum", [P, 1]), p.sb("x2_root", [P, 1]), p.sb("x2_scale", [P, 1])
        pY, pF, pM, pN = (p.banks(n, 1) for n in ("y_rows", "fox_T", "mem_T", "yn_T"))
        pP, pX = p.banks("products", 2), p.banks("merged_T", 2)
        s_w, s_gain = p.sem("w_in_sbuf"), p.sem("gain_in_sbuf")
        s_in, s_x2 = p.sems("tile_in_sbuf", 2), p.sems("x2_done", 2)
        s_y, s_f, s_m, s_ynT, s_mT = (p.sem(n) for n in ("y_turned", "fox_turned", "mem_turned", "yn_turned", "merged_turned"))
        s_fk, s_mk, s_silu, s_mk2 = (p.sem(n) for n in ("foxT_kept", "memT_kept", "silu", "mergedT_kept"))
        s_ln, s_std, s_yn = p.sem("ln_step"), p.sem("ln_root"), p.sem("y_normed")
        s_prod, s_used = p.sem("product"), p.sems("product_read", 2)
        s_gate, s_sq, s_root, s_h, s_h2 = (p.sem(n) for n in ("gate_step", "x2_squares", "x2_root", "h2_step", "h2"))
        s_open = p.sem("opened")
        s_rstd, s_x2a = p.sem("ln_scale"), p.sem("x2_first_half")
        s_x2out, s_h2out = p.sem("x2_stored"), p.sem("h2_stored")
        x_p = io["x_prompt"][0].rearrange("(t p) d -> t p d", p=P)
        y_view = scr["y"].rearrange("j p t -> p j t")

        p.start()
        with nc.Block() as block:
            @block.sync
            def _(sp):
                for buf, src in ((fox, scr["fox"][0]), (mem, scr["mem"][0]), (y, y_view[:, :, 0:P]), (gates, scr["gates"][0]), (x, x_p[0])):
                    sp.dma_start(buf[0][:], src).then_inc(s_in[0], 16)
                for n in ("w_fox_o", "w_mem_o", "w_conv_o"):
                    sp.dma_start(w[n][:], io[n][0].rearrange("(k p) n -> p k n", p=P)).then_inc(s_w, 16)
                sp.dma_start(w_out[:], io["w_out"][0].rearrange("(k p) n -> p k n", p=P)).then_inc(s_w, 16)
                sp.dma_start(gain[:], io["norm2_w"][0].partition_broadcast(P)).then_inc(s_gain, 16)

                def load(T):
                    n = SAM if T.sample else P
                    b = T.b
                    sp.wait_ge(s_x2[b], S0 + T.u)
                    sp.dma_start(fox[b][0:n, :], scr["fox"][T.n, 0:n, :]).then_inc(s_in[b], 16)
                    sp.dma_start(mem[b][0:n, :], scr["mem"][T.n, 0:n, :]).then_inc(s_in[b], 16)
                    sp.dma_start(y[b][:, :, 0:n], y_view[:, :, SEQ + HIST:] if T.sample else y_view[:, :, bass.ts(T.n, P)])\
                        .then_inc(s_in[b], 16)
                    sp.dma_start(gates[b][0:n, :], scr["gates"][T.n, 0:n, :]).then_inc(s_in[b], 16)
                    sp.dma_start(x[b][0:n, :], io["x_sample"][0] if T.sample else x_p[T.n]).then_inc(s_in[b], 16)

                def emit(T):
                    n = SAM if T.sample else P
                    if not T.last:
                        load(T.next())
                    sp.wait_ge(s_x2[T.b], S0 + T.u + 1)
                    sp.dma_start(scr["x2"][T.n, 0:n, :], x2[0:n, :]).then_inc(s_x2out, 16)
                    sp.wait_ge(s_h2, S0 + T.n + 1)
                    sp.dma_start(scr["h2"][T.n, 0:n, :], h2[0:n, :]).then_inc(s_h2out, 16)
                    if T.sample:
                        sp.dma_start(scr["x2"][T.n, n:P, :], x2[0:n, :]).then_inc(s_x2out, 16)
                        sp.dma_start(scr["h2"][T.n, n:P, :], h2[0:n, :]).then_inc(s_h2out, 16)
                all_tiles(sp, emit)
                sp.wait_ge(s_x2out, S0 + 16 * (NT + 2))
                sp.wait_ge(s_h2out, S0 + 16 * (NT + 2))

            n_in = 5

            @block.tensor
            def _(pe):
                def turn_branches(T):
                    n, N = (SAM if T.sample else P), T.n
                    pe.wait_ge(s_in[T.b], S0 + 16 * n_in * (T.u + 1))
                    pe.wait_ge(s_yn, S0 + N)
                    for j in range(CT):
                        ins = pe.transpose(pY[0:n, 0, j * P:(j + 1) * P], y[T.b][:, j, 0:n], c.ident[:])
                    ins.then_inc(s_y, 1)
                    for src, bank, kept, done in ((fox, pF, s_fk, s_f), (mem, pM, s_mk, s_m)):
                        pe.wait_ge(kept, S0 + N)
                        for k in range(BK):
                            ins = pe.transpose(bank[:, 0, k * P:k * P + n], src[T.b][0:n, k * P:(k + 1) * P], c.ident[0:n, 0:n])
                        ins.then_inc(done, 1)

                def emit(T):
                    n, N = (SAM if T.sample else P), T.n
                    pe.wait_ge(s_yn, S0 + N + 1)
                    pe.wait_ge(s_silu, S0 + N)
                    for k in range(BK):
                        ins = pe.transpose(pN[:, 0, k * P:k * P + n], yn[0:n, k * P:(k + 1) * P], c.ident[0:n, 0:n])
                    ins.then_inc(s_ynT, 1)
                    if isinstance(T.u, int) or T.b == 0:
                        pe.wait_ge(s_w, S0 + 64)
                    for b, (name, wn, ready) in enumerate((("fox", "w_fox_o", s_fk), ("mem", "w_mem_o", s_mk), ("conv", "w_conv_o", s_silu))):
                        pe.wait_ge(ready, S0 + N + 1)
                        for h in range(2):
                            pe.wait_ge(s_used[h], S0 + 4 * N + b)
                            for k in range(BK):
                                ins = pe.matmul(pP[0:n, h, :], turned[name][:, k, 0:n], w[wn][:, k, h * BANK:(h + 1) * BANK],
                                                start=(k == 0), stop=(k == BK - 1))
                            ins.then_inc(s_prod, 1)
                    if not T.last:
                        turn_branches(T.next())
                    pe.wait_ge(s_gate, S0 + 2 * 5 * N + 10)
                    pe.wait_ge(s_mk2, S0 + N)
                    for k in range(KC):
                        ins = pe.transpose(pX[:, k // 4, (k % 4) * P:(k % 4) * P + n], m[0:n, k * P:(k + 1) * P], c.ident[0:n, 0:n])
                    ins.then_inc(s_mT, 1)
                    pe.wait_ge(s_mk2, S0 + N + 1)
                    for h in range(2):
                        pe.wait_ge(s_used[h], S0 + 4 * N + 3)
                        for k in range(KC):
                            ins = pe.matmul(pP[0:n, h, :], mT[:, k, 0:n], w_out[:, k, h * BANK:(h + 1) * BANK],
                                            start=(k == 0), stop=(k == KC - 1))
                        ins.then_inc(s_prod, 1)
                turn_branches(Tile(0, 0))
                all_tiles(pe, emit)

            @block.scalar
            def _(act):
                def keep_branches(T):
                    n, N = (SAM if T.sample else P), T.n
                    for name, bank, ready, kept in (("fox", pF, s_f, s_fk), ("mem", pM, s_m, s_mk)):
                        act.wait_ge(ready, S0 + N + 1)
                        act.activation(turned[name][:, :, 0:n], bank[:, 0, :].rearrange("p (k t) -> p k t", t=P)[:, :, 0:n], ACT.Copy)\
                           .then_inc(kept, 1)
                    act.wait_ge(s_ln, S0 + 2 * N + 2)
                    act.wait_ge(s_yn, S0 + N)
                    act.activation(std[0:n, :], mv[0:n, 1:2], ACT.Sqrt, bias=c.eps[0:n, 0:1]).then_inc(s_std, 1)

                def emit(T):
                    n, N = (SAM if T.sample else P), T.n
                    act.wait_ge(s_ynT, S0 + N + 1)
                    act.wait_ge(s_prod, S0 + 8 * N)
                    for k in range(BK):
                        ins = act.activation(turned["conv"][:, k, 0:n], pN[:, 0, k * P:k * P + n], ACT.Silu,
                                             scale=c.vec[:, V_LNW + k:V_LNW + k + 1], bias=c.vec[:, V_LNB + k:V_LNB + k + 1])
                    ins.then_inc(s_silu, 1)
                    if not T.last:
                        act.wait_ge(s_prod, S0 + 8 * N + 4)
                        keep_branches(T.next())
                    act.wait_ge(s_mT, S0 + N + 1)
                    act.wait_ge(s_prod, S0 + 8 * N)
                    act.activation(mT[:, :, 0:n], pX[:].rearrange("p a (k t) -> p (a k) t", t=P)[:, :, 0:n], ACT.Copy).then_inc(s_mk2, 1)
                    act.wait_ge(s_x2[T.b], S0 + T.u + 1)
                    act.wait_ge(s_h2, S0 + N)
                    act.wait_ge(s_sq, S0 + N)
                    act.activation(junk[0:n, :], x2[0:n, :], ACT.Square, accum_out=ss[0:n, :]).then_inc(s_sq, 1)
                    act.wait_ge(s_sq, S0 + N + 1)
                    act.activation(root[0:n, :], ss[0:n, :], ACT.Sqrt, scale=1.0 / D, bias=c.eps[0:n, 0:1]).then_inc(s_root, 1)
                keep_branches(Tile(0, 0))
                all_tiles(act, emit)

            @block.vector
            def _(dve):
                def norm_y(T):
                    n, N = (SAM if T.sample else P), T.n
                    dve.wait_ge(s_y, S0 + N + 1)
                    dve.wait_ge(s_std, S0 + N)
                    dve.bn_stats(stats[0:n, :], pY[0:n, 0, :]).then_inc(s_ln, 1)
                    dve.wait_ge(s_ln, S0 + 2 * N + 1)
                    dve.sem_inc(s_open, 1)
                    dve.bn_aggr(mv[0:n, :], stats[0:n, :]).then_inc(s_ln, 1)
                    dve.wait_ge(s_std, S0 + N + 1)
                    dve.reciprocal(rstd[0:n, :], std[0:n, :]).then_inc(s_rstd, 1)
                    dve.wait_ge(s_rstd, S0 + N + 1)
                    dve.wait_ge(s_ynT, S0 + N)
                    dve.tensor_scalar(yn[0:n, :], pY[0:n, 0, :], mv[0:n, 0:1], rstd[0:n, 0:1], ALU.subtract, ALU.mult)\
                       .then_inc(s_yn, 1)

                def emit(T):
                    n, N, b = (SAM if T.sample else P), T.n, T.b
                    dve.wait_ge(s_in[b], S0 + 16 * n_in * (T.u + 1))
                    dve.wait_ge(s_mT, S0 + N)
                    step = 10 * N
                    for br, (g_at, use) in enumerate(((0, 0), (2, 1), (1, 2))):
                        for h in range(2):
                            cols = slice(h * BANK, (h + 1) * BANK)
                            dst = m if br == 0 else part
                            dve.wait_ge(s_prod, S0 + 8 * N + 2 * br + h + 1)
                            ins = dve.tensor_tensor(dst[0:n, cols], pP[0:n, h, :],
                                                    gates[b][0:n, g_at * D + h * BANK:g_at * D + (h + 1) * BANK], ALU.mult)
                            ins.then_inc(s_gate, 1)
                            step = step + 1
                            dve.wait_ge(s_gate, S0 + step)
                            dve.sem_inc(s_used[h], 1)
                            if br:
                                dve.tensor_tensor(m[0:n, cols], m[0:n, cols], part[0:n, cols], ALU.add).then_inc(s_gate, 1)
                                step = step + 1
                                dve.wait_ge(s_gate, S0 + step)
                    if not T.last:
                        norm_y(T.next())
                    dve.wait_ge(s_x2out, S0 + 16 * N)
                    for h in range(2):
                        cols = slice(h * BANK, (h + 1) * BANK)
                        dve.wait_ge(s_prod, S0 + 8 * N + 6 + h + 1)
                        ins = dve.tensor_tensor(x2[0:n, cols], pP[0:n, h, :], x[b][0:n, cols], ALU.add)
                        if h:
                            ins.then_inc(s_x2[b], 1)
                            dve.wait_ge(s_x2[b], S0 + T.u + 1)
                        else:
                            ins.then_inc(s_x2a, 1)
                            dve.wait_ge(s_x2a, S0 + N + 1)
                        dve.sem_inc(s_used[h], 1)
                    dve.wait_ge(s_root, S0 + N + 1)
                    dve.reciprocal(inv[0:n, :], root[0:n, :]).then_inc(s_h, 1)
                    dve.wait_ge(s_h, S0 + N + 1)
                    dve.wait_ge(s_h2out, S0 + 16 * N)
                    dve.scalar_tensor_tensor(h2[0:n, :], x2[0:n, :], inv[0:n, 0:1], gain[0:n, :], ALU.mult, ALU.mult).then_inc(s_h2, 1)

                dve.wait_ge(s_gain, S0 + 16)
                norm_y(Tile(0, 0))
                all_tiles(dve, emit)


U_RING, V_RING = 8, 16
ROUND = 2 * TOPK
GROUP = 4
TURNS = NH // 2


class Turn:

    def __init__(self, t, hp):
        self.sample = t is SAMPLE
        self.steps = TOPK // 2 if self.sample else TOPK
        self.number = TURNS * t + hp
        if self.sample:
            self.before = ROUND * TURNS * NT + 2 * self.steps * hp
            self.u_uses = ROUND // U_RING * TURNS * NT + 2 * self.steps // U_RING * hp
            self.v_uses = ROUND // V_RING * TURNS * NT + 2 * self.steps // V_RING * hp
            self.groups = ROUND // GROUP * TURNS * NT + 2 * self.steps // GROUP * hp
        else:
            B = self.number
            self.before, self.groups = ROUND * B, ROUND // GROUP * B
            self.u_uses, self.v_uses = ROUND // U_RING * B, ROUND // V_RING * B
        self.out = SAM if self.sample else P

    def done(self, q):
        return ROUND + self.before + self.steps * (q + 1)


def experts(nc, io, scr, c):
    with Phase(nc, "peer") as p:
        wq = p.sb("w_q", [P, KC, NH * 2 * NK])
        keysT = p.sb("keys_T", [P, 2 * NH, NK])
        u = [p.sb(f"u_rows{k}", [P, D]) for k in range(U_RING)]
        v = [p.sb(f"v_rows{k}", [P, D]) for k in range(V_RING)]
        h2n, h2 = p.sb("h2_next", [P, D]), p.sb("h2", [P, D])
        h2T = p.sb("h2_next_T", [P, KC, P])
        x2, y = p.sb("x2", [P, D]), p.sb("y", [P, D])
        idx = p.sb("expert_idx", [P, 2, TOPK], U32)
        g = p.sb("expert_gate", [P, 2, TOPK])
        twins = p.sb("twin_identity", [P, SAM])
        twin_idx, twin_g = p.sb("twin_idx", [P, 2, TOPK // 2], U32), p.sb("twin_gate", [P, 2, TOPK // 2])
        dots, gl, wt = ([p.sb(f"{n}{q}", [P, TOPK]) for q in range(2)] for n in ("dots", "gelu", "weights"))
        diag = [p.sb(f"diag{k}", [P, P]) for k in range(GROUP)]
        qs, qT = p.sb("q", [P, 2 * NK]), p.sb("q_T", [P, 2, P])
        sc, rep = p.sb("side_scores", [P, 2, NK]), p.sb("side_rest", [P, 2, NK])
        top, topi, topf = p.sb("side_top", [P, 2, TOPK]), p.sb("side_idx", [P, 2, TOPK], U32), p.sb("side_idx_f", [P, 2, TOPK])
        cand, crest = p.sb("pairs", [P, TOPK * TOPK]), p.sb("pairs_rest", [P, TOPK * TOPK])
        best, pos = p.sb("best", [P, TOPK]), p.sb("best_pos", [P, TOPK], U32)
        split, splitf = p.sb("pos_split", [P, 2, TOPK], U32), p.sb("pos_split_f", [P, 2, TOPK])
        hot, pick = p.sb("one_hot", [P, 2 * TOPK * TOPK]), p.sb("picked", [P, 2 * TOPK])
        iota = p.sb("iota", [P, TOPK])
        ebias, ex, esum, einv = p.sb("exp_bias", [P, 1]), p.sb("exps", [P, TOPK]), p.sb("exp_sum", [P, 1]), p.sb("exp_scale", [P, 1])
        acc, pQ, pQT, pS, pH = p.banks("acc", 2), p.banks("q", 1), p.banks("q_T", 1), p.banks("scores", 1), p.banks("h2_T", 2)
        s_w, s_keys, s_kturn, s_kkeep, s_iota = (p.sem(n) for n in ("wq_in_sbuf", "keys_in_sbuf", "keys_turned", "keysT_kept", "iota"))
        s_u, s_v = p.sems("u_gathered", U_RING, start=0), p.sems("v_gathered", V_RING, start=0)
        s_dot, s_sum, s_diag = p.sem("dots"), p.sem("sums"), p.sem("diagonals")
        s_gelu, s_wt = p.sem("gelu"), p.sem("weights")
        s_h2n, s_hcopy, s_hturn, s_hT = (p.sem(n) for n in ("h2_in_sbuf", "h2_copied", "h2_turned", "h2T_kept"))
        s_x2, s_init, s_y, s_yout = (p.sem(n) for n in ("x2_in_sbuf", "sum_started", "y_rows", "y_stored"))
        s_q, s_qk, s_qt, s_qtk, s_sc = (p.sem(n) for n in ("q", "q_kept", "q_turned", "qT_kept", "side_scores"))
        s_route, s_eb, s_ex, s_done = (p.sem(n) for n in ("route_step", "exp_bias", "exps", "routed"))
        s_twins, s_parted = p.sem("twins"), p.sem("twins_parted")
        s_carry = p.sem("wait_carried")
        s_pcarry = p.sem("pool_wait_carried")
        ROUTE_AT = (0, 4, 6)
        ROUTE = 26
        y_p = io["y_prompt"][0].rearrange("(t p) d -> t p d", p=P)

        def tiles(eng, start, queries, turn, end):
            queries(0)
            turn(None, 0, 0)
            with eng.Fori(0, NT) as t:
                start(t)
                with eng.Fori(0, TURNS - 1) as hp:
                    T = Turn(t, hp)
                    turn(T, 2 * T.number + 2, 2 * hp + 2)
                queries(t + 1)
                T = Turn(t, TURNS - 1)
                turn(T, 2 * T.number + 2, 0)
                end(t)
            start(SAMPLE)
            with eng.Fori(0, TURNS - 1) as hp:
                T = Turn(SAMPLE, hp)
                turn(T, 2 * T.number + 2, 2 * hp + 2)
            turn(Turn(SAMPLE, TURNS - 1), None, None)
            end(SAMPLE)

        nothing = lambda t: None

        def sample_head(T, q):
            return 2 * (T.number - TURNS * NT) + q

        p.start()
        with nc.Block() as block:
            @block.sync
            def _(sp):
                for s, name in enumerate(("peer_keys1", "peer_keys2")):
                    sp.dma_start(u[s][:].rearrange("p (h d) -> p h d", h=NH), io[name][0].rearrange("h k d -> k h d")).then_inc(s_keys, 16)
                sp.dma_start(h2n[:], scr["h2"][0]).then_inc(s_h2n, 16)
                for q in range(4):
                    n = NH * 2 * NK // 4
                    sp.dma_start(wq[:, :, q * n:(q + 1) * n], io["peer_w_q"][0, :, q * n:(q + 1) * n].rearrange("(k p) n -> p k n", p=P))\
                      .then_inc(s_w, 16)
                sp.dma_start(x2[:], scr["x2"][0]).then_inc(s_x2, 16)
                with sp.Fori(0, NT) as t:
                    sp.wait_ge(s_hturn, S0 + t + 1)
                    sp.wait_ge(s_hcopy, S0 + t + 1)
                    sp.dma_start(h2n[:], scr["h2"][t + 1]).then_inc(s_h2n, 16)
                    sp.wait_ge(s_init, S0 + t + 1)
                    sp.dma_start(x2[:], scr["x2"][t + 1]).then_inc(s_x2, 16)
                    sp.wait_ge(s_y, S0 + t + 1)
                    sp.dma_start(y_p[t], y[:]).then_inc(s_yout, 16)
                sp.wait_ge(s_y, S0 + NT + 1)
                sp.dma_start(io["y_sample"][0], y[0:SAM, :]).then_inc(s_yout, 16)
                sp.wait_ge(s_yout, S0 + 16 * (NT + 1))

            @block.gpsimd
            def _(pool):
                pool.iota(iota[:], pattern=[[1, TOPK]], base=0, channel_multiplier=0,
                          allow_small_or_imprecise_dtypes=True).then_inc(s_iota, 1)

                def turn(T, R, head):
                    if T is None:
                        return
                    for q in range(2):
                        pool.wait_ge(s_done, S0 + 2 * T.number + q + 1)
                        if T.sample:
                            pool.wait_ge(s_parted, S0 + 4 * (sample_head(T, q) + 1))
                        rows = twin_idx if T.sample else idx
                        for j in range(T.steps):
                            at = T.steps * q + j
                            for rows_of, table, ring, used in ((u, "peer_u", s_u, s_dot), (v, "peer_v", s_v, s_sum)):
                                k = at % len(ring)
                                pool.wait_ge(used, S0 + ROUND + T.before + at - len(ring) + 1)
                                pool.sem_inc(s_pcarry, 1)
                                pool.indirect_dma_start(rows_of[k][:], None, io[table][0],
                                                        bass.IndirectOffsetOnAxis(ap=rows[:, q, j:j + 1], axis=0)).then_inc(ring[k], 16)
                pool.wait_ge(s_kturn, S0 + NH)
                tiles(pool, nothing, nothing, turn, nothing)

            @block.tensor
            def _(pe):
                for h in range(NH):
                    if h == 0:
                        pe.wait_ge(s_keys, S0 + 32)
                    if h >= 2:
                        pe.wait_ge(s_kkeep, S0 + h - 1)
                    for s in range(2):
                        ins = pe.transpose(pH[:, h % 2, s * P:(s + 1) * P], u[s][:, h * P:(h + 1) * P], c.ident[:])
                    ins.then_inc(s_kturn, 1)
                pe.wait_ge(s_kkeep, S0 + NH)
                pe.wait_ge(s_w, S0 + 64)
                pe.sem_inc(s_sum, ROUND)

                def start(t):
                    rows = SAM if t is SAMPLE else P
                    pe.wait_ge(s_x2, S0 + 16 * (t + 1))
                    pe.wait_ge(s_y, S0 + t)
                    for h in range(2):
                        ins = pe.matmul(acc[0:rows, h, :], c.ident[:, 0:rows], x2[:, h * BANK:(h + 1) * BANK],
                                        start=True, stop=True)
                    ins.then_inc(s_init, 1)

                def queries(t):
                    pe.wait_ge(s_h2n, S0 + 16 * (t + 1))
                    pe.wait_ge(s_hT, S0 + t)
                    for k in range(KC):
                        ins = pe.transpose(pH[:, k // 4, (k % 4) * P:(k % 4 + 1) * P], h2n[:, k * P:(k + 1) * P], c.ident[:])
                    ins.then_inc(s_hturn, 1)
                    pe.wait_ge(s_hT, S0 + t + 1)

                def route(R, head, part):
                    if part == 0:
                        pe.wait_ge(s_qk, S0 + R)
                        for k in range(KC):
                            ins = pe.matmul(pQ[:, 0, 0:2 * NK], h2T[:, k, :], wq[:, k, bass.ts(head, 2 * NK)],
                                            start=(k == 0), stop=(k == KC - 1))
                        ins.then_inc(s_q, 1)
                    elif part == 1:
                        pe.wait_ge(s_qk, S0 + R + 1)
                        pe.wait_ge(s_qtk, S0 + R)
                        for s in range(2):
                            ins = pe.transpose(pQT[:, 0, s * P:(s + 1) * P], qs[:, s * NK:(s + 1) * NK], c.ident[:])
                        ins.then_inc(s_qt, 1)
                    else:
                        pe.wait_ge(s_qtk, S0 + R + 1)
                        pe.wait_ge(s_done, S0 + R)
                        for s in range(2):
                            ins = pe.matmul(pS[:, 0, s * NK:(s + 1) * NK], qT[:, s, :],
                                            keysT[:, bass.ds(2 * head + s, 1), :].rearrange("p o k -> p (o k)"), start=True, stop=True)
                        ins.then_inc(s_sc, 1)

                def turn(T, R, head):
                    for q in range(2):
                        if T is None:
                            for part in range(3):
                                route(R + q, head + q, part)
                            continue
                        for j in range(T.steps):
                            at = T.steps * q + j
                            if R is not None and j in ROUTE_AT:
                                route(R + q, head + q, ROUTE_AT.index(j))
                            pe.wait_ge(s_diag, S0 + ROUND + T.before + at + 1)
                            pe.wait_ge(s_v[at % V_RING], 16 * (T.v_uses + at // V_RING + 1))
                            for h in range(2):
                                ins = pe.matmul(acc[0:T.out, h, :], diag[at % GROUP][:, 0:T.out], v[at % V_RING][:, h * BANK:(h + 1) * BANK],
                                                start=False, stop=False, skip_group_check=True)
                            ins.then_inc(s_sum, 1)
                tiles(pe, start, queries, turn, nothing)

            @block.scalar
            def _(act):
                for h in range(NH):
                    act.wait_ge(s_kturn, S0 + h + 1)
                    act.activation(keysT[:, 2 * h:2 * h + 2, :], pH[:, h % 2, 0:2 * P].rearrange("p (s k) -> p s k", s=2), ACT.Copy)\
                       .then_inc(s_kkeep, 1)
                act.sem_inc(s_diag, ROUND)
                act.wait_ge(s_twins, S0 + 1)

                def queries(t):
                    act.wait_ge(s_hturn, S0 + t + 1)
                    act.wait_ge(s_q, S0 + NH * t)
                    act.activation(h2T[:], pH[:].rearrange("p a (k t) -> p (a k) t", t=P), ACT.Copy).then_inc(s_hT, 1)

                def route(R, part):
                    if part == 0:
                        act.wait_ge(s_q, S0 + R + 1)
                        act.wait_ge(s_qt, S0 + R)
                        act.activation(qs[:], pQ[:, 0, 0:2 * NK], ACT.Copy).then_inc(s_qk, 1)
                    elif part == 1:
                        act.wait_ge(s_qt, S0 + R + 1)
                        act.wait_ge(s_sc, S0 + R)
                        act.activation(qT[:], pQT[:, 0, 0:2 * P].rearrange("p (s t) -> p s t", s=2), ACT.Copy).then_inc(s_qtk, 1)
                    else:
                        act.wait_ge(s_eb, S0 + R + 1)
                        act.wait_ge(s_done, S0 + R)
                        act.activation(ex[:], best[:], ACT.Exp, bias=ebias[:, 0:1], accum_out=esum[:]).then_inc(s_ex, 1)

                def turn(T, R, head):
                    for q in range(2):
                        if T is None:
                            for part in range(3):
                                route(R + q, part)
                            continue
                        for k in range(T.steps // GROUP):
                            at = T.steps * q + GROUP * k
                            cols = slice(GROUP * k, GROUP * (k + 1))
                            act.wait_ge(s_dot, S0 + ROUND + T.before + at + GROUP)
                            act.activation(gl[q][:, cols], dots[q][:, cols], ACT.Gelu).then_inc(s_gelu, 1)
                            act.wait_ge(s_wt, S0 + T.groups + T.steps // GROUP * q + k + 1)
                            for j in range(GROUP):
                                act.wait_ge(s_sum, S0 + ROUND + T.before + at + j - GROUP + 1)
                                eye = twins[:] if T.sample else c.ident[:]
                                act.activation(diag[j][:, 0:T.out], eye, ACT.Copy,
                                               scale=wt[q][:, GROUP * k + j:GROUP * k + j + 1]).then_inc(s_diag, 1)
                            if R is not None and k < 2:
                                route(R + q, k)
                        if R is not None:
                            route(R + q, 2)

                def end(t):
                    rows = SAM if t is SAMPLE else P
                    done = ROUND * TURNS * (t + 1) if t is not SAMPLE else ROUND * TURNS * NT + TOPK * TURNS
                    act.wait_ge(s_sum, S0 + ROUND + done)
                    act.wait_ge(s_yout, S0 + 16 * t)
                    act.activation(y[0:rows, :], acc[0:rows, :, :].rearrange("p a n -> p (a n)"), ACT.Copy).then_inc(s_y, 1)
                tiles(act, nothing, queries, turn, end)

            @block.vector
            def _(dve):
                dve.sem_inc(s_dot, ROUND)
                dve.wait_ge(s_iota, S0 + 1)

                dve.tensor_tensor(twins[:], c.ident[:, 0:SAM], c.ident[:, SAM:P], ALU.add).then_inc(s_twins, 1)

                def start(t):
                    dve.wait_ge(s_dot, S0 + ROUND + ROUND * TURNS * t)
                    dve.wait_ge(s_h2n, S0 + 16 * (t + 1))
                    dve.tensor_copy(h2[:], h2n[:]).then_inc(s_hcopy, 1)
                    if t is SAMPLE:
                        for q in range(2):
                            part(q, q)
                    dve.wait_ge(s_hcopy, S0 + t + 1)
                    carry()

                def carry():
                    dve.sem_inc(s_carry, 1)

                def route(R, q, former):
                    s = Chain(dve, s_route)
                    s.n = ROUTE * R
                    dve.wait_ge(s_sc, S0 + R + 1)
                    s.link(dve.tensor_copy(sc[:], pS[:, 0, 0:2 * NK].rearrange("p (s k) -> p s k", s=2)))
                    carry()
                    for i in range(2):
                        s.step(dve.max(top[:, i, 0:8], sc[:, i, :]))
                    s.wait()
                    carry()
                    for i in range(2):
                        s.step(dve.match_replace(rep[:, i, :], top[:, i, 0:8], sc[:, i, :], LOWEST))
                        s.step(dve.max_index(topi[:, i, 0:8], top[:, i, 0:8], sc[:, i, :]))
                    s.wait()
                    carry()
                    for i in range(2):
                        s.step(dve.max(top[:, i, 8:16], rep[:, i, :]))
                    s.wait()
                    carry()
                    for i in range(2):
                        s.step(dve.max_index(topi[:, i, 8:16], top[:, i, 8:16], rep[:, i, :]))
                    sq = lambda ap: ap.rearrange("p (a b) -> p a b", a=TOPK)
                    s.wait()
                    s.step(dve.tensor_copy(topf[:], topi[:]))
                    s.link(dve.tensor_tensor(sq(cand[:]), top[:, 0, :].unsqueeze(2).broadcast_to([P, TOPK, TOPK]),
                                             top[:, 1, :].unsqueeze(1).broadcast_to([P, TOPK, TOPK]), ALU.add))
                    carry()
                    s.link(dve.max(best[:, 0:8], cand[:]))
                    carry()
                    s.step(dve.match_replace(crest[:], best[:, 0:8], cand[:], LOWEST))
                    s.link(dve.max_index(pos[:, 0:8], best[:, 0:8], cand[:]))
                    carry()
                    s.step(dve.max(best[:, 8:16], crest[:]))
                    dve.tensor_scalar(ebias[:], best[:, 0:1], -1.0, None, ALU.mult).then_inc(s_eb, 1)
                    s.wait()
                    carry()
                    s.link(dve.max_index(pos[:, 8:16], best[:, 8:16], crest[:]))
                    s.step(dve.tensor_scalar(split[:, 0, :], pos[:], 4, None, ALU.logical_shift_right))
                    s.link(dve.tensor_scalar(split[:, 1, :], pos[:], TOPK - 1, None, ALU.bitwise_and))
                    s.link(dve.tensor_copy(splitf[:], split[:]))
                    flat = splitf[:].rearrange("p s j -> p (s j)")
                    s.link(dve.tensor_tensor(hot[:].rearrange("p (m a) -> p m a", a=TOPK), flat.unsqueeze(2).broadcast_to([P, 2 * TOPK, TOPK]),
                                             iota[:].unsqueeze(1).broadcast_to([P, 2 * TOPK, TOPK]), ALU.is_equal))
                    hot4 = hot[:].rearrange("p (s j a) -> p s j a", s=2, a=TOPK)
                    s.link(dve.tensor_tensor(hot4, hot4, topf[:].unsqueeze(2).broadcast_to([P, 2, TOPK, TOPK]), ALU.mult))
                    s.link(dve.tensor_reduce(pick[:], hot[:].rearrange("p (m a) -> p m a", a=TOPK), AX, ALU.add))
                    if former is not None:
                        dve.wait_ge(s_sum, S0 + former.done(q))
                    s.step(dve.scalar_tensor_tensor(idx[:, q, :], pick[:, 0:TOPK], float(NK), pick[:, TOPK:], ALU.mult, ALU.add))
                    dve.wait_ge(s_ex, S0 + R + 1)
                    s.link(dve.reciprocal(einv[:], esum[:]))
                    dve.tensor_scalar(g[:, q, :], ex[:], einv[:, 0:1], None, ALU.mult).then_inc(s_done, 1)
                    assert s.taken == ROUTE, s.taken

                def part(n, q):
                    dve.wait_ge(s_done, S0 + 2 * TURNS * NT + n + 1)
                    half = TOPK // 2
                    for dst, src in ((twin_idx, idx), (twin_g, g)):
                        dve.tensor_copy(dst[0:SAM, q, :], src[0:SAM, q, 0:half]).then_inc(s_parted, 1)
                        dve.tensor_copy(dst[SAM:P, q, :], src[SAM:P, q, half:]).then_inc(s_parted, 1)

                def turn(T, R, head):
                    for q in range(2):
                        if T is not None:
                            gates = twin_g if T.sample else g
                            if T.sample:
                                dve.wait_ge(s_parted, S0 + 4 * (sample_head(T, q) + 1))
                            else:
                                dve.wait_ge(s_done, S0 + 2 * T.number + q + 1)
                            for j in range(T.steps):
                                at = T.steps * q + j
                                k = at % U_RING
                                dve.wait_ge(s_u[k], 16 * (T.u_uses + at // U_RING + 1))
                                dve.tensor_tensor_reduce(u[k][:], u[k][:], h2[:], 1.0, 0.0, ALU.mult, ALU.add,
                                                         dots[q][:, j:j + 1]).then_inc(s_dot, 1)
                                if j % GROUP == GROUP - 1:
                                    n = j // GROUP
                                    cols = slice(GROUP * n, GROUP * (n + 1))
                                    dve.wait_ge(s_gelu, S0 + T.groups + T.steps // GROUP * q + n + 1)
                                    dve.tensor_tensor(wt[q][:, cols], gl[q][:, cols], gates[:, q, cols], ALU.mult).then_inc(s_wt, 1)
                        if R is not None:
                            route(R + q, q, T)
                            if T is not None and T.sample:
                                carry()
                                part(sample_head(T, q) + 2, q)
                tiles(dve, start, nothing, turn, nothing)


OUTS = (("y_prompt", (1, SEQ, D)), ("y_sample", (1, SAM, D)),
        ("fox_k_prompt", (1, 1, SEQ, HF, DF)), ("fox_v_prompt", (1, 1, SEQ, HF, DF)), ("fox_logf_prompt", (1, 1, SEQ, HF)),
        ("conv_prompt", (1, 1, HIST, DC)),
        ("mem_k_prompt", (1, 1, NMEM, HM, DM)), ("mem_v_prompt", (1, 1, NMEM, HM, DM)),
        ("fox_k_sample", (1, 1, SAM, HF, DF)), ("fox_v_sample", (1, 1, SAM, HF, DF)), ("fox_logf_sample", (1, 1, SAM, HF)),
        ("conv_sample", (1, 1, HIST, DC)))


class Constants:
    pass


def build(nc, io, phases=99):
    scr = {name: nc.dram_tensor(f"scr_{name}", shape, F32).ap() for name, shape in (
        ("xT", (NT + 1, P, D)), ("qT", (HF, DF + 2, TOK)), ("kT", (HF, DF + 2, PAST + TOK)),
        ("mqT", (HM, DM, TOK)), ("mkT", (2, HM, DM, NMEM)), ("a", (TOK, DC)), ("gates", (NT + 1, P, GATES)),
        ("y", (CT, P, CONV_OUT)), ("fox", (NT + 1, P, HF * DF)), ("mem", (NT + 1, P, HM * DM)),
        ("x2", (NT + 1, P, D)), ("h2", (NT + 1, P, D)))}
    with ExitStack() as stack:
        c = Constants()
        c.ident = stack.enter_context(nc.sbuf_tensor("identity", [P, P], F32))
        c.vec = stack.enter_context(nc.sbuf_tensor("feature_vectors", [P, V_ROWS], F32))
        c.causal = stack.enter_context(nc.sbuf_tensor("causal_mask", [P, P], F32))
        c.eps = stack.enter_context(nc.sbuf_tensor("eps", [P, 1], F32))
        front(nc, io, scr, c, phases)
        if phases > 4:
            forgetting_attention(nc, io, scr, c)
            memory_attention(nc, io, scr, c)
        if phases > 5:
            merge(nc, io, scr, c)
        if phases > 6:
            experts(nc, io, scr, c)


def front(nc, io, scr, c, phases):
    with ExitStack() as stack:
        c.aT = stack.enter_context(nc.sbuf_tensor("conv_input_T", [P, CT, 2 * HIST + SEQ + SAM], F32))
        c.dw = stack.enter_context(nc.sbuf_tensor("conv_taps", [P, CT, CW], F32))
        c.forget = stack.enter_context(nc.sbuf_tensor("forget_logits", [P, NT + 1, HF], F32))
        constants(nc, io, scr, c)
        rows = lambda name: io[name].rearrange("l b (t p) h d -> (l b t) p (h d)", p=P)
        mem_k, mem_v = rows("mem_k_prompt"), rows("mem_v_prompt")
        mem_x = io["mem_prompt"][0].rearrange("(t p) d -> t p d", p=P)
        project(nc, c, "memkv", lambda T: mem_x[T.n], V_MEMNORM, io["w_mem_kv"][0], [
            Chunk("mk", "norm", 0, 0, HM * DM, head=DM, gain=io["mem_k_norm"][0], rows_out=lambda T: mem_k[T.n],
                  turn=P, turned_out=lambda T: scr["mkT"][0, :, :, bass.ts(T.n, P)].rearrange("h d t -> d h t")),
            Chunk("mv", "copy", 1, HM * DM, HM * DM, rows_out=lambda T: mem_v[T.n]),
        ], memory_tiles)
        if phases < 2:
            return
        x_p = io["x_prompt"][0].rearrange("(t p) d -> t p d", p=P)
        k_p, v_p = rows("fox_k_prompt"), rows("fox_v_prompt")
        k_s, v_s = (io[n][0, 0].rearrange("t h d -> t (h d)") for n in ("fox_k_sample", "fox_v_sample"))
        a_t = scr["a"].rearrange("(t p) n -> t p n", p=P)
        heads_T = lambda name, at: scr[name][:, 0:DF, at].rearrange("h d t -> d h t")
        F = HF * DF
        project(nc, c, "in", lambda T: io["x_sample"][0] if T.sample else x_p[T.n], V_NORM1, io["w_in"][0], [
            Chunk("q", "norm", 0, 0, F, head=DF, gain=io["fox_q_norm"][0], turn=DF,
                  turned_out=lambda T: heads_T("qT", bass.ts(T.n, P))),
            Chunk("k", "norm", 1, F, F, head=DF, gain=io["fox_k_norm"][0], rows_out=lambda T: k_s if T.sample else k_p[T.n], turn=DF,
                  turned_out=lambda T: heads_T("kT", slice(SEQ + PAST, SEQ + PAST + P) if T.sample else bass.ts(T.n, P))),
            Chunk("mq", "norm", 2, C_MQ, HM * DM, head=DM, gain=io["mem_q_norm"][0], turn=P,
                  turned_out=lambda T: scr["mqT"][:, :, bass.ts(T.n, P)].rearrange("h d t -> d h t")),
            Chunk("v", "copy", 0, 2 * F, F, rows_out=lambda T: v_s if T.sample else v_p[T.n]),
            Chunk("ga", "glu", 1, C_GLU, DC, rows_out=lambda T: a_t[T.n][0:SAM] if T.sample else a_t[T.n], turn=P),
            Chunk("gb", "glu_gate", 2, C_GLU + DC, DC),
            Chunk("f", "forget", 0, 3 * F, HF),
        ], all_tiles, xT_out=lambda T: scr["xT"][T.n], forget=c.forget,
            a_cols=lambda T: (c.aT[:, :, 2 * HIST + SEQ:] if T.sample else c.aT[:, :, bass.ds(HIST + T.n * P, P)]))
        if phases < 3:
            return
        decay(nc, io, scr, c)
        gates_and_conv(nc, io, scr, c)


INS = ("x_prompt", "x_sample", "mem_prompt", "cache_fox_k", "cache_fox_v", "cache_fox_logf", "cache_conv",
       "cache_mem_k", "cache_mem_v", "norm1_w", "w_in", "b_forget", "fox_q_norm", "fox_k_norm", "w_fox_o",
       "w_dw", "b_dw", "conv_ln_w", "conv_ln_b", "w_conv_o", "mem_norm_w", "w_mem_kv", "mem_q_norm", "mem_k_norm",
       "w_mem_o", "w_out", "norm2_w", "peer_w_q", "peer_keys1", "peer_keys2", "peer_u", "peer_v")


def kernel(**inputs):
    import numpy as _np
    import concourse.bacc as _bacc
    from concourse import mybir as _mybir
    from concourse.bass_utils import run_bass_kernel_spmd as _run

    nc = _bacc.Bacc("TRN2", target_bir_lowering=False, num_devices=1)
    arrays, io = {}, {}
    for name in INS:
        a = _np.ascontiguousarray(inputs[name])
        arrays[f"in_{name}"] = a
        io[name] = nc.dram_tensor(f"in_{name}", a.shape, _mybir.dt.from_np(a.dtype), kind="ExternalInput").ap()
    for name, shape in OUTS:
        io[name] = nc.dram_tensor(f"out_{name}", shape, F32, kind="ExternalOutput").ap()
    build(nc, io)
    r = _run(nc, [arrays], core_ids=[0])
    return tuple(r.results[0][f"out_{name}"] for name, _ in OUTS)
```

```python
from contextlib import ExitStack

import concourse.bass as bass
from concourse import mybir

F32 = mybir.dt.float32
F32R = mybir.dt.float32r
U32 = mybir.dt.uint32
ALU = mybir.AluOpType
ACT = mybir.ActivationFunctionType
AX = mybir.AxisListType.X

P = 128
D = 1024
KC = D // P
SEQ = 1024
NT = SEQ // P
SAM = 64
SAMPLE = NT
PAST = 512
TOK = SEQ + P
HF, DF = 8, 64
HM, DM = 4, 128
NMEM = 256
DC = 512
CT = DC // P
CW = 31
HIST = CW - 1
NH, NK, TOPK = 8, 128, 16
EPS = 1e-6
MASKED = -1e30
LOWEST = -3.4e38
C_GLU = 3 * HF * DF + HF
C_MQ = C_GLU + 2 * DC
C_G = C_MQ + HM * DM
GATES = 3 * D
S0 = 1
BANK = 512
CONV_OUT = SEQ + HIST + SAM


class Tile:

    def __init__(self, u, b, sample=False, last=False):
        self.u, self.b, self.sample, self.last = u, b, sample, last
        self.n = 2 * u + b

    def next(self):
        if self.b == 0:
            return Tile(self.u, 1)
        return Tile(self.u + 1, 0, sample=self.before_sample)

    before_sample = False


def all_tiles(eng, emit):
    with eng.Fori(0, NT // 2 - 1) as u:
        emit(Tile(u, 0))
        emit(Tile(u, 1))
    emit(Tile(NT // 2 - 1, 0))
    end = Tile(NT // 2 - 1, 1)
    end.before_sample = True
    emit(end)
    emit(Tile(NT // 2, 0, sample=True, last=True))


all_tiles.count = NT + 1


def memory_tiles(eng, emit):
    emit(Tile(0, 0))
    emit(Tile(0, 1, last=True))


memory_tiles.count = NMEM // P


class Chain:

    def __init__(self, eng, sem):
        self.eng, self.sem, self.n = eng, sem, 0
        self.taken = 0

    def step(self, ins):
        ins.then_inc(self.sem, 1)
        self.n = self.n + 1
        self.taken += 1
        return ins

    def wait(self):
        self.eng.wait_ge(self.sem, S0 + self.n)

    def link(self, ins):
        self.step(ins)
        self.wait()


class Phase:

    def __init__(self, nc, tag):
        self.nc, self.tag, self.started = nc, tag, []
        self.stack = ExitStack()

    def __enter__(self):
        self.stack.enter_context(self.nc.cleanup_on_exit())
        return self

    def __exit__(self, *a):
        return self.stack.__exit__(*a)

    def sb(self, name, shape, dt=F32):
        return self.stack.enter_context(self.nc.sbuf_tensor(f"{self.tag}_{name}", shape, dt))

    def banks(self, name, n):
        return self.stack.enter_context(self.nc.psum_tensor(f"{self.tag}_{name}_ps", [P, n, BANK], F32))

    def sem(self, name, start=S0):
        sem = self.nc.alloc_semaphore(name=f"{self.tag}_{name}")
        if start:
            self.started.append(sem)
        return sem

    def start(self):
        engines = (self.nc.sync, self.nc.gpsimd, self.nc.scalar, self.nc.tensor, self.nc.vector)
        for k, sem in enumerate(self.started):
            engines[k % len(engines)].sem_inc(sem, S0)
        self.nc.all_engine_barrier()

    def sems(self, name, n, start=S0):
        return [self.sem(f"{name}{i}", start) for i in range(n)]


class Weights:

    def __init__(self, phase, parts, pieces=1):
        self.parts, self.pieces = parts, pieces
        self.buf = {n: phase.sb(n, [P, a.shape[0] // P, a.shape[1]]) for n, a in parts.items()}
        self.ready = {n: phase.sem(f"{n}_in_sbuf") for n in parts}
        self.left = [(n, k) for n in parts for k in range(pieces)]
        phase.start()

    def load(self, sp, count=None):
        count = len(self.left) if count is None else count
        now, self.left = self.left[:count], self.left[count:]
        for n, k in now:
            rows = self.buf[n].shape[1] // self.pieces
            sp.dma_start(self.buf[n][:, k * rows:(k + 1) * rows, :],
                         self.parts[n].rearrange("(k p) n -> p k n", p=P)[:, k * rows:(k + 1) * rows, :]).then_inc(self.ready[n], 16)



V_NORM1, V_MEMNORM, V_LNW, V_LNB, V_BDW, V_ROWS = 0, 8, 16, 20, 24, 28


def constants(nc, io, scr, c):
    with Phase(nc, "const") as p:
        rows = p.sb("vec_rows", [V_ROWS, P])
        dw = p.sb("dw_rows", [CW, DC])
        hist = p.sb("hist_rows", [HIST, DC])
        ps = p.banks("ps_const", 3)
        loaded, zeroed, made, turned, kept = (p.sem(n) for n in ("c_loaded", "c_zeroed", "c_made", "c_turned", "c_kept"))
        p.start()
        with nc.Block() as block:
            @block.sync
            def _(sp):
                for at, name, n in ((V_NORM1, "norm1_w", 8), (V_MEMNORM, "mem_norm_w", 8), (V_LNW, "conv_ln_w", 4),
                                    (V_LNB, "conv_ln_b", 4), (V_BDW, "b_dw", 4)):
                    sp.dma_start(rows[at:at + n, :], io[name][0].rearrange("(n p) -> n p", p=P)).then_inc(loaded, 16)
                sp.dma_start(dw[:], io["w_dw"][0]).then_inc(loaded, 16)
                sp.dma_start(hist[:], io["cache_conv"][0, 0]).then_inc(loaded, 16)
                sp.wait_ge(loaded, S0 + 7 * 16)

            @block.gpsimd
            def _(pool):
                pool.memset(c.ident[:], 0.0).then_inc(zeroed, 1)
                pool.memset(c.causal[:], 0.0).then_inc(zeroed, 1)
                pool.wait_ge(zeroed, S0 + 2)
                pool.affine_select(out=c.ident[:], in_=c.ident[:], compare_op=ALU.not_equal, fill=1.0, base=0,
                                   pattern=[[-1, P]], channel_multiplier=1).then_inc(made, 1)
                pool.affine_select(out=c.causal[:], in_=c.causal[:], compare_op=ALU.is_ge, fill=MASKED, base=0,
                                   pattern=[[-1, P]], channel_multiplier=1).then_inc(made, 1)

            @block.tensor
            def _(pe):
                pe.wait_ge(loaded, S0 + 7 * 16)
                pe.wait_ge(made, S0 + 1)
                pe.transpose(ps[:, 0, 0:V_ROWS], rows[:], c.ident[0:V_ROWS, 0:V_ROWS]).then_inc(turned, 1)
                for j in range(CT):
                    pe.transpose(ps[:, 1, j * CW:(j + 1) * CW], dw[:, j * P:(j + 1) * P], c.ident[0:CW, 0:CW]).then_inc(turned, 1)
                    pe.transpose(ps[:, 2, j * HIST:(j + 1) * HIST], hist[:, j * P:(j + 1) * P],
                                 c.ident[0:HIST, 0:HIST]).then_inc(turned, 1)

            @block.vector
            def _(dve):
                dve.memset(c.aT[:, :, 0:HIST], 0.0).then_inc(kept, 1)
                dve.memset(c.eps[:], EPS).then_inc(kept, 1)
                dve.wait_ge(turned, S0 + 1 + 2 * CT)
                dve.tensor_copy(c.vec[:], ps[:, 0, 0:V_ROWS]).then_inc(kept, 1)
                dve.tensor_copy(c.dw[:], ps[:, 1, 0:CT * CW].rearrange("p (j k) -> p j k", j=CT)).then_inc(kept, 1)
                dve.tensor_copy(c.aT[:, :, HIST + SEQ:2 * HIST + SEQ],
                                ps[:, 2, 0:CT * HIST].rearrange("p (j k) -> p j k", j=CT)).then_inc(kept, 1)
                dve.wait_ge(kept, S0 + 5)


class Chunk:

    def __init__(self, name, kind, bank, src, width, head=0, gain=None, rows_out=None, turn=None, turned_out=None):
        self.name, self.kind, self.bank, self.src, self.width = name, kind, bank, src, width
        self.head, self.gain, self.rows_out, self.turn, self.turned_out = head, gain, rows_out, turn, turned_out


def project(nc, c, tag, x_tile, vec0, w, chunks, tiles, xT_out=None, forget=None, a_cols=None, ahead=None):
    with Phase(nc, tag) as p:
        x = [p.sb(f"x{b}", [P, D]) for b in range(2)]
        xT = [p.sb(f"xT{b}", [P, KC, P]) for b in range(2)]
        junk = p.sb(f"junk", [P, D])
        ssx, rx = p.sb(f"ssx", [P, 1]), p.sb(f"rx", [P, 1])
        norms = [ch for ch in chunks if ch.kind == "norm"]
        turns = [ch for ch in chunks if ch.turn]
        squares = {ch.name: p.sb(f"sq_{ch.name}", [P, BANK]) for ch in norms}
        sums = {ch.name: p.sb(f"ss_{ch.name}", [P, BANK // ch.head]) for ch in norms}
        scales = {ch.name: p.sb(f"rs_{ch.name}", [P, BANK // ch.head]) for ch in norms}
        gains = {ch.name: p.sb(f"gain_{ch.name}", [P, ch.head]) for ch in norms}
        rows = {ch.name: p.sb(f"rows_{ch.name}", [P, BANK]) for ch in chunks if ch.kind != "forget"}
        stage = {ch.name: p.sb(f"turned_{ch.name}", [ch.turn, BANK // ch.turn, P]) for ch in turns if ch.turned_out}
        pT, pC, pX, pY = p.banks(f"pT", 2), p.banks(f"pC", 3), p.banks(f"pX", 2), p.banks(f"pY", 1)
        s_gain, s_zero = p.sem("gains_in_sbuf"), p.sem("x_pad_zeroed")
        s_x = p.sems("x_in_sbuf", 2)
        s_ssx, s_rx, s_rxi, s_xn = (p.sem(n) for n in ("x_squares", "x_root", "x_scale", "x_normed"))
        s_xturn, s_xT = p.sems("x_turned", 2), p.sem("xT_in_sbuf")
        s_xTout = p.sems("xT_stored", 2)
        s_chunk = p.sems("chunk_done", 2)
        s_free = [p.sem(f"bank{k}_read") for k in range(3)]
        s_open = p.sem("turn_opened")
        s_sq, s_ss, s_rs, s_rsi, s_z1 = (p.sem(f"head_{n}") for n in ("squares", "sums", "roots", "scales", "scaled"))
        s_rows = {ch.name: p.sem(f"{ch.name}_rows_ready") for ch in chunks}
        s_rout = {ch.name: p.sem(f"{ch.name}_rows_stored") for ch in chunks if ch.rows_out}
        s_turn = {ch.name: p.sem(f"{ch.name}_turned") for ch in turns}
        s_keep = {ch.name: p.sem(f"{ch.name}T_in_sbuf") for ch in turns}
        s_tout = {ch.name: p.sem(f"{ch.name}T_stored") for ch in turns if ch.turned_out}
        n_chunks, n_norms = len(chunks), len(norms)
        users = {k: [ch for ch in chunks if ch.bank == k] for k in range(3)}
        x_users = [ch for ch in turns if ch.turn == DF]
        y_users = [ch for ch in turns if ch.turn == P]

        def before(ch):
            line = x_users if ch.turn == DF else y_users
            k = line.index(ch)
            return (line[k - 1], 0) if k else (line[-1], 1)

        def bank_of(ch):
            return (pX[0:DF, :, :].rearrange("p a (h t) -> p (a h) t", t=P) if ch.turn == DF
                    else pY[:, 0, :].rearrange("p (h t) -> p h t", t=P))

        p.start()
        with nc.Block() as block:
            @block.sync
            def _(sp):
                sp.dma_start(x[0][:], x_tile(Tile(0, 0))).then_inc(s_x[0], 16)
                for ch in norms:
                    sp.dma_start(gains[ch.name][:], ch.gain.partition_broadcast(P)).then_inc(s_gain, 16)
                w.load(sp)
                if ahead is not None:
                    ahead.load(sp, 3)

                def load(T):
                    n = SAM if T.sample else P
                    sp.wait_ge(s_xturn[T.b], S0 + T.u)
                    sp.dma_start(x[T.b][0:n, :], x_tile(T)).then_inc(s_x[T.b], 16)

                def emit(T):
                    n = SAM if T.sample else P
                    if not T.last:
                        load(T.next())
                    if xT_out is not None:
                        sp.wait_ge(s_xT, S0 + T.n + 1)
                        sp.dma_start(xT_out(T), xT[T.b][:].rearrange("p k t -> p (k t)")).then_inc(s_xTout[T.b], 16)
                    for ch in chunks:
                        if ch.rows_out:
                            sp.wait_ge(s_rows[ch.name], S0 + T.n + 1)
                            sp.dma_start(ch.rows_out(T), rows[ch.name][0:n, :]).then_inc(s_rout[ch.name], 16)
                    for ch in turns:
                        if ch.turned_out:
                            sp.wait_ge(s_keep[ch.name], S0 + T.n + 1)
                            sp.dma_start(ch.turned_out(T), stage[ch.name][:]).then_inc(s_tout[ch.name], 16)

                tiles(sp, emit)
                if xT_out is not None:
                    sp.wait_ge(s_xTout[0], S0 + 16 * ((tiles.count + 1) // 2))
                    sp.wait_ge(s_xTout[1], S0 + 16 * (tiles.count // 2))
                for s in list(s_rout.values()) + list(s_tout.values()):
                    sp.wait_ge(s, S0 + 16 * tiles.count)

            @block.scalar
            def _(act):
                def square(T):
                    act.wait_ge(s_x[T.b], S0 + 16 * (T.u + 1))
                    if T.sample:
                        act.wait_ge(s_zero, S0 + 1)
                    act.wait_ge(s_rx, S0 + T.n)
                    act.wait_ge(s_ssx, S0 + T.n)
                    act.activation(junk[:], x[T.b][:], ACT.Square, accum_out=ssx[:]).then_inc(s_ssx, 1)
                    act.wait_ge(s_ssx, S0 + T.n + 1)
                    act.wait_ge(s_xn, S0 + T.n)
                    act.activation(rx[:], ssx[:], ACT.Sqrt, scale=1.0 / D, bias=c.eps[:, 0:1]).then_inc(s_rx, 1)

                def keep_xT(T):
                    act.wait_ge(s_xturn[T.b], S0 + T.u + 1)
                    if xT_out is not None:
                        act.wait_ge(s_xTout[T.b], S0 + 16 * T.u)
                    act.wait_ge(s_chunk[T.b], S0 + n_chunks * T.u)
                    for k in range(KC):
                        ins = act.activation(xT[T.b][:, k, :], pT[:, k // 4, (k % 4) * P:(k % 4 + 1) * P], ACT.Copy,
                                             scale=c.vec[:, vec0 + k:vec0 + k + 1])
                    ins.then_inc(s_xT, 1)

                def emit(T):
                    if not T.last:
                        square(T.next())
                    for k, ch in enumerate(chunks):
                        if ch.kind == "norm":
                            act.wait_ge(s_chunk[T.b], S0 + n_chunks * T.u + k + 1)
                            act.wait_ge(s_ss, S0 + n_norms * T.n + norms.index(ch))
                            act.activation(squares[ch.name][:], pC[:, ch.bank, :], ACT.Square).then_inc(s_sq, 1)
                            act.wait_ge(s_ss, S0 + n_norms * T.n + norms.index(ch) + 1)
                            act.wait_ge(s_z1, S0 + n_norms * T.n + norms.index(ch))
                            act.activation(scales[ch.name][:], sums[ch.name][:], ACT.Sqrt, scale=1.0 / ch.head,
                                           bias=c.eps[:, 0:1]).then_inc(s_rs, 1)
                            if ch is norms[-1] and not T.last:
                                keep_xT(T.next())
                        if ch.kind == "glu_gate":
                            act.wait_ge(s_chunk[T.b], S0 + n_chunks * T.u + k + 1)
                            act.wait_ge(s_rows["ga"], S0 + T.n)
                            act.activation(rows[ch.name][:], pC[:, ch.bank, :], ACT.Sigmoid).then_inc(s_rows[ch.name], 1)
                    for ch in turns:
                        act.wait_ge(s_turn[ch.name], S0 + T.n + 1)
                        if ch.turned_out:
                            act.wait_ge(s_tout[ch.name], S0 + 16 * T.n)
                            act.activation(stage[ch.name][:], bank_of(ch), ACT.Copy).then_inc(s_keep[ch.name], 1)
                        else:
                            n = SAM if T.sample else P
                            act.activation(a_cols(T), bank_of(ch)[:, :, 0:n], ACT.Copy).then_inc(s_keep[ch.name], 1)
                square(Tile(0, 0))
                keep_xT(Tile(0, 0))
                tiles(act, emit)

            @block.tensor
            def _(pe):
                def turn_x(T):
                    pe.wait_ge(s_xn, S0 + T.n + 1)
                    pe.wait_ge(s_xT, S0 + T.n)
                    for k in range(KC):
                        ins = pe.transpose(pT[:, k // 4, (k % 4) * P:(k % 4 + 1) * P], x[T.b][:, k * P:(k + 1) * P], c.ident[:])
                    ins.then_inc(s_xturn[T.b], 1)

                def emit(T):
                    pe.wait_ge(s_xT, S0 + T.n + 1)
                    for ch in chunks:
                        if isinstance(T.u, int) or T.b == 0:
                            pe.wait_ge(w.ready[ch.name], S0 + 16)
                        line = users[ch.bank]
                        pe.wait_ge(s_free[ch.bank], S0 + len(line) * T.n + line.index(ch))
                        for k in range(KC):
                            ins = pe.matmul(pC[:, ch.bank, 0:ch.width], xT[T.b][:, k, :],
                                            w.buf[ch.name][:, k, :], start=(k == 0), stop=(k == KC - 1))
                        ins.then_inc(s_chunk[T.b], 1)
                        if ch.kind == "copy" and not T.last:
                            turn_x(T.next())
                    for ch in turns:
                        pe.wait_ge(s_rows[ch.name], S0 + T.n + 1)
                        prev, back = before(ch)
                        pe.wait_ge(s_keep[prev.name], S0 + T.n + 1 - back)
                        pe.sem_inc(s_open, 1)
                        for h in range(BANK // ch.turn):
                            ins = pe.transpose(bank_of(ch)[:, h, :], rows[ch.name][:, h * ch.turn:(h + 1) * ch.turn], c.ident[:])
                        ins.then_inc(s_turn[ch.name], 1)
                turn_x(Tile(0, 0))
                tiles(pe, emit)

            @block.vector
            def _(dve):
                def norm_x(T):
                    dve.wait_ge(s_rx, S0 + T.n + 1)
                    dve.wait_ge(s_x[T.b], S0 + 16 * (T.u + 1))
                    dve.reciprocal(rx[:], rx[:]).then_inc(s_rxi, 1)
                    dve.wait_ge(s_rxi, S0 + T.n + 1)
                    dve.tensor_scalar(x[T.b][:], x[T.b][:], rx[:, 0:1], None, ALU.mult).then_inc(s_xn, 1)

                def emit(T):
                    n = T.n
                    if not T.last:
                        N = T.next()
                        if N.sample:
                            dve.wait_ge(s_xturn[N.b], S0 + N.u)
                            dve.memset(x[N.b][SAM:P, :], 0.0).then_inc(s_zero, 1)
                            dve.wait_ge(s_zero, S0 + 1)
                        norm_x(N)
                    for k, ch in enumerate(chunks):
                        if ch.kind == "norm":
                            m = norms.index(ch)
                            H = BANK // ch.head
                            heads = lambda ap: ap.rearrange("p (h d) -> p h d", d=ch.head)
                            dve.wait_ge(s_sq, S0 + n_norms * n + m + 1)
                            dve.wait_ge(s_rs, S0 + n_norms * n + m)
                            dve.tensor_reduce(sums[ch.name][:], heads(squares[ch.name][:]), AX, ALU.add).then_inc(s_ss, 1)
                            dve.wait_ge(s_rs, S0 + n_norms * n + m + 1)
                            dve.reciprocal(scales[ch.name][:], scales[ch.name][:]).then_inc(s_rsi, 1)
                            dve.wait_ge(s_rsi, S0 + n_norms * n + m + 1)
                            if ch.turn:
                                dve.wait_ge(s_turn[ch.name], S0 + n)
                            if ch.rows_out:
                                dve.wait_ge(s_rout[ch.name], S0 + 16 * n)
                            dve.tensor_tensor(heads(rows[ch.name][:]), heads(pC[:, ch.bank, :]),
                                              scales[ch.name][:].unsqueeze(2).broadcast_to([P, H, ch.head]), ALU.mult)\
                               .then_inc(s_z1, 1)
                            dve.wait_ge(s_z1, S0 + n_norms * n + m + 1)
                            dve.sem_inc(s_free[ch.bank], 1)
                            dve.tensor_tensor(heads(rows[ch.name][:]), heads(rows[ch.name][:]),
                                              gains[ch.name][:].unsqueeze(1).broadcast_to([P, H, ch.head]),
                                              ALU.mult).then_inc(s_rows[ch.name], 1)
                        elif ch.kind == "copy":
                            dve.wait_ge(s_chunk[T.b], S0 + n_chunks * T.u + k + 1)
                            dve.wait_ge(s_rout[ch.name], S0 + 16 * n)
                            dve.tensor_copy(rows[ch.name][:], pC[:, ch.bank, :]).then_inc(s_rows[ch.name], 1)
                            dve.wait_ge(s_rows[ch.name], S0 + n + 1)
                            dve.sem_inc(s_free[ch.bank], 1)
                        elif ch.kind == "glu_gate":
                            a = next(o for o in chunks if o.name == "ga")
                            dve.wait_ge(s_rows[ch.name], S0 + n + 1)
                            dve.wait_ge(s_rout["ga"], S0 + 16 * n)
                            dve.wait_ge(s_turn["ga"], S0 + n)
                            dve.tensor_tensor(rows["ga"][:], pC[:, a.bank, :], rows[ch.name][:], ALU.mult).then_inc(s_rows["ga"], 1)
                            dve.wait_ge(s_rows["ga"], S0 + n + 1)
                            dve.sem_inc(s_free[a.bank], 1)
                            dve.sem_inc(s_free[ch.bank], 1)
                        elif ch.kind == "forget":
                            dve.wait_ge(s_chunk[T.b], S0 + n_chunks * T.u + k + 1)
                            dve.tensor_copy(forget[:, T.n, :], pC[:, ch.bank, 0:ch.width]).then_inc(s_rows[ch.name], 1)
                            dve.wait_ge(s_rows[ch.name], S0 + n + 1)
                            dve.sem_inc(s_free[ch.bank], 1)
                dve.wait_ge(s_gain, S0 + 16 * n_norms)
                norm_x(Tile(0, 0))
                tiles(dve, emit)


def decay(nc, io, scr, c, ahead):
    NC = PAST // P
    with Phase(nc, "decay") as p:
        bias = p.sb("forget_bias", [P, HF])
        t, e, l, logf = (p.sb(n, [P, NT + 1, HF]) for n in ("decay_t", "decay_e", "decay_l", "decay_logf"))
        lT = p.sb("logf_T", [HF, TOK])
        cum = p.sb("cum_T", [HF, TOK])
        zeros = p.sb("scan_zeros", [HF, TOK])
        ones_row = p.sb("ones_row", [HF, PAST + TOK])
        past = p.sb("past_logf", [P, NC, HF])
        past_T = p.sb("past_T", [HF, PAST])
        suffix = p.sb("suffix_T", [HF, PAST])
        key_row = p.sb("key_row", [HF, PAST + TOK])
        query_row = p.sb("query_row", [HF, TOK])
        ck = p.sb("cached_k", [P, NC, HF * DF])
        ckT = p.sb("cached_kT", [DF, 2, HF, P])
        cm = p.sb("cached_mk", [P, NMEM // P, HM * DM])
        cmT = p.sb("cached_mkT", [P, 2, HM, P])
        pL = p.banks("p_logf", 3)
        pP = p.banks("p_past", 1)
        pK = p.banks("p_keys", 4)
        loaded, keys_loaded, stored, key_stored = p.sem("d_loaded"), p.sem("d_keys_loaded"), p.sem("d_stored"), p.sems("cached_keys_stored", 2)
        abs_, exp_, log_, done = (p.sem(n) for n in ("d_abs", "d_exp", "d_log", "d_logf"))
        turned, past_turned, pkeys, kept = (p.sem(n) for n in ("d_turned", "d_past_turned", "d_keys_turned", "d_keys_kept"))
        v, rows_ready = p.sem("d_vector_step"), p.sem("d_rows_ready")
        p.start()
        with nc.Block() as block:
            @block.sync
            def _(sp):
                sp.dma_start(bias[:], io["b_forget"][0].partition_broadcast(P)).then_inc(loaded, 16)
                sp.dma_start(past[:], io["cache_fox_logf"][0, 0].rearrange("(t p) h -> p t h", p=P)).then_inc(loaded, 16)
                sp.dma_start(ck[:], io["cache_fox_k"][0, 0].rearrange("(t p) h d -> p t (h d)", p=P)).then_inc(keys_loaded, 16)
                sp.dma_start(cm[:], io["cache_mem_k"][0, 0].rearrange("(t p) h d -> p t (h d)", p=P)).then_inc(keys_loaded, 16)
                for i in range(NC):
                    sp.wait_ge(kept, S0 + i + 1)
                    sp.dma_start(scr["kT"][:, 0:DF, SEQ + i * P:SEQ + (i + 1) * P].rearrange("h d t -> d h t"),
                                 ckT[:, i % 2, :, :]).then_inc(key_stored[i % 2], 16)
                for i in range(NMEM // P):
                    sp.wait_ge(kept, S0 + NC + i + 1)
                    sp.dma_start(scr["mkT"][1, :, :, i * P:(i + 1) * P].rearrange("h d t -> d h t"),
                                 cmT[:, i % 2, :, :]).then_inc(stored, 16)
                sp.wait_ge(done, S0 + 1)
                sp.dma_start(io["fox_logf_prompt"][0, 0].rearrange("(t p) h -> p t h", p=P), logf[:, 0:NT, :]).then_inc(stored, 16)
                sp.dma_start(io["fox_logf_sample"][0, 0], logf[0:SAM, NT, :]).then_inc(stored, 16)
                sp.wait_ge(rows_ready, S0 + 1)
                sp.dma_start(scr["kT"][:, DF, :], key_row[:]).then_inc(stored, 16)
                sp.dma_start(scr["kT"][:, DF + 1, :], ones_row[:]).then_inc(stored, 16)
                sp.dma_start(scr["qT"][:, DF, :], ones_row[:, 0:TOK]).then_inc(stored, 16)
                sp.dma_start(scr["qT"][:, DF + 1, :], query_row[:]).then_inc(stored, 16)
                ahead.load(sp)
                sp.dma_start(io["conv_prompt"][0, 0], scr["a"][SEQ - HIST:SEQ, :]).then_inc(stored, 16)
                sp.dma_start(io["conv_sample"][0, 0], scr["a"][SEQ + SAM - HIST:SEQ + SAM, :]).then_inc(stored, 16)
                sp.wait_ge(stored, S0 + 16 * (NMEM // P + 8))
                for b in range(2):
                    sp.wait_ge(key_stored[b], S0 + 16 * NC // 2)

            @block.scalar
            def _(act):
                act.wait_ge(abs_, S0 + 1)
                act.activation(e[:], e[:], ACT.Exp, scale=-1.0).then_inc(exp_, 1)
                act.wait_ge(exp_, S0 + 1)
                act.activation(l[:], e[:], ACT.Ln, bias=1.0).then_inc(log_, 1)
                for i in range(NC):
                    act.wait_ge(pkeys, S0 + i + 1)
                    if i >= 2:
                        act.wait_ge(key_stored[i % 2], S0 + 16 * (i // 2))
                    act.activation(ckT[:, i % 2, :, :], pK[0:DF, 2 * (i % 2):2 * (i % 2) + 2, :].rearrange("p a (h t) -> p (a h) t", t=P),
                                   ACT.Copy).then_inc(kept, 1)
                for i in range(NMEM // P):
                    act.wait_ge(pkeys, S0 + NC + i + 1)
                    act.activation(cmT[:, i % 2, :, :], pK[:, 2 * (i % 2), :].rearrange("p (h t) -> p h t", t=P),
                                   ACT.Copy).then_inc(kept, 1)

            @block.tensor
            def _(pe):
                pe.wait_ge(loaded, S0 + 32)
                for i in range(NC):
                    ins = pe.transpose(pP[0:HF, 0, i * P:(i + 1) * P], past[:, i, :], c.ident[:])
                ins.then_inc(past_turned, 1)
                pe.wait_ge(done, S0 + 1)
                for i in range(NT + 1):
                    ins = pe.transpose(pL[0:HF, i // 4, (i % 4) * P:(i % 4 + 1) * P], logf[:, i, :], c.ident[:])
                ins.then_inc(turned, 1)
                pe.wait_ge(keys_loaded, S0 + 32)
                for i in range(NC):
                    if i >= 2:
                        pe.wait_ge(kept, S0 + i - 1)
                    for h in range(HF):
                        ins = pe.transpose(pK[0:DF, 2 * (i % 2) + h // 4, (h % 4) * P:(h % 4 + 1) * P],
                                           ck[:, i, h * DF:(h + 1) * DF], c.ident[:])
                    ins.then_inc(pkeys, 1)
                for i in range(NMEM // P):
                    pe.wait_ge(kept, S0 + NC + i - 1)
                    for h in range(HM):
                        ins = pe.transpose(pK[:, 2 * (i % 2), h * P:(h + 1) * P], cm[:, i, h * P:(h + 1) * P], c.ident[:])
                    ins.then_inc(pkeys, 1)

            @block.vector
            def _(dve):
                s = Chain(dve, v)
                s.step(dve.memset(zeros[:], 0.0))
                s.step(dve.memset(ones_row[:], 1.0))
                dve.wait_ge(loaded, S0 + 32)
                s.link(dve.tensor_tensor(t[:], c.forget[:], bias[:].unsqueeze(1).broadcast_to([P, NT + 1, HF]), ALU.add))
                s.link(dve.tensor_scalar(e[:], t[:], -1.0, None, ALU.mult))
                dve.tensor_tensor(e[:], e[:], t[:], ALU.max).then_inc(abs_, 1)
                dve.wait_ge(log_, S0 + 1)
                dve.scalar_tensor_tensor(logf[:], t[:], 0.0, l[:], ALU.min, ALU.subtract).then_inc(done, 1)
                dve.wait_ge(past_turned, S0 + 1)
                s.link(dve.tensor_copy(past_T[:], pP[0:HF, 0, :][:, ::-1]))
                s.link(dve.tensor_tensor_scan(suffix[:], past_T[:], zeros[:, 0:PAST], 0.0, ALU.add, ALU.add))
                s.link(dve.tensor_tensor(suffix[:], suffix[:], past_T[:], ALU.subtract))
                s.link(dve.tensor_scalar(key_row[:, SEQ:SEQ + PAST], suffix[:, ::-1], float(DF) ** 0.5, None, ALU.mult))
                dve.wait_ge(turned, S0 + 1)
                s.link(dve.tensor_copy(lT[:, 0:SEQ], pL[0:HF, 0:2, :].rearrange("p a t -> p (a t)")))
                s.link(dve.tensor_copy(lT[:, SEQ:TOK], pL[0:HF, 2, 0:P]))
                s.link(dve.tensor_tensor_scan(cum[:, 0:SEQ], lT[:, 0:SEQ], zeros[:, 0:SEQ], 0.0, ALU.add, ALU.add))
                s.link(dve.tensor_tensor_scan(cum[:, SEQ:TOK], lT[:, SEQ:TOK], zeros[:, SEQ:TOK], 0.0, ALU.add, ALU.add))
                s.link(dve.tensor_scalar(query_row[:], cum[:], float(DF) ** 0.5, None, ALU.mult))
                s.link(dve.tensor_scalar(key_row[:, 0:SEQ], cum[:, 0:SEQ], -float(DF) ** 0.5, None, ALU.mult))
                dve.tensor_scalar(key_row[:, SEQ + PAST:], cum[:, SEQ:TOK], -float(DF) ** 0.5, None, ALU.mult).then_inc(rows_ready, 1)


def gates_and_conv(nc, io, scr, c, w):
    NG, TILES = GATES // BANK, NT + 1
    X_RING = 3
    raw, ready = w.buf["gates"], w.ready["gates"]
    with Phase(nc, "gates") as p:
        xh, xl = (p.sb(f"x_T_{n}", [P, TILES, KC, P], F32R) for n in ("upper", "lower"))
        upper, lower = ([p.sb(f"w_{n}{b}", [P, KC, BANK], F32R) for b in range(2)] for n in ("upper", "lower"))
        x = [p.sb(f"x_T{b}", [P, KC, P]) for b in range(X_RING)]
        g = p.sb("gate_rows", [P, 3, BANK])
        y = [p.sb(f"conv_y{b}", [P, CONV_OUT]) for b in range(CT)]
        ps = p.banks("p_gates", 3)
        s_x, s_xh, s_xl = p.sems("gate_xT_in_sbuf", X_RING), p.sem("x_upper"), p.sem("x_lower")
        s_wh, s_wl = p.sems("w_upper", 2), p.sems("w_lower", 2)
        s_prod, s_sig, s_open = p.sem("gate_product"), p.sem("gate_sigmoid"), p.sem("gate_wait_carried")
        s_out = p.sems("gates_stored", 3)
        tap, y_done, y_out = p.sem("conv_tap"), p.sem("conv_done"), p.sem("conv_stored")

        def over_tiles(eng, emit):
            with eng.Fori(0, NT // 2) as u:
                for b in range(2):
                    emit(2 * u + b, b, u)
            emit(SAMPLE, 2, 0)

        def uses(n, bank, u):
            return n + u if bank == 2 else NT // 2 * n + u

        def split_upper(copy, b):
            copy(upper[b][:], raw[:]).then_inc(s_wh[b], 1)

        def split_lower(eng, b):
            eng.tensor_tensor(lower[b][:], raw[:], upper[b][:].bitcast(F32), ALU.subtract).then_inc(s_wl[b], 1)

        p.start()
        with nc.Block() as block:
            @block.sync
            def _(sp):
                for t in range(TILES):
                    if t >= X_RING:
                        sp.wait_ge(s_xl, S0 + t - X_RING + 1)
                    sp.dma_start(x[t % X_RING][:].rearrange("p k n -> p (k n)"), scr["xT"][t]).then_inc(s_x[t % X_RING], 16)

                def chunk(n, b, i, last=False):
                    if not last:
                        sp.wait_ge(s_wl[b], S0 + i + 1)
                        cols = bass.ds((n + 1) * BANK + C_G, BANK)
                        sp.dma_start(raw[:], io["w_in"][0, :, cols].rearrange("(k p) n -> p k n", p=P)).then_inc(ready, 16)

                    def store(t, bank, u):
                        sp.wait_ge(s_sig, S0 + TILES * n + t + 3)
                        sp.dma_start(scr["gates"][t, :, bass.ds(n * BANK, BANK)], g[:, bank, :]).then_inc(s_out[bank], 16)
                    over_tiles(sp, store)

                with sp.Fori(0, NG // 2 - 1) as i:
                    for b in range(2):
                        chunk(2 * i + b, b, i)
                for j in range(CT):
                    sp.wait_ge(y_done, S0 + j + 1)
                    sp.dma_start(scr["y"][j], y[j][:]).then_inc(y_out, 16)
                for b in range(2):
                    chunk(NG - 2 + b, b, NG // 2 - 1, last=b == 1)
                sp.wait_ge(y_out, S0 + 16 * CT)
                for k in range(3):
                    sp.wait_ge(s_out[k], S0 + 16 * uses(NG, k, 0))

            @block.gpsimd
            def _(pool):
                for n in range(1, NG):
                    b, i = n % 2, n // 2
                    pool.wait_ge(ready, S0 + 16 * (n + 1))
                    if i:
                        pool.wait_ge(s_prod, S0 + TILES * (n - 1))
                    split_upper(pool.tensor_copy, b)
                    pool.wait_ge(s_wh[b], S0 + i + 1)
                    split_lower(pool, b)

            @block.tensor
            def _(pe):
                with pe.Fori(0, NG // 2) as i:
                    for b in range(2):
                        n = 2 * i + b

                        pe.wait_ge(s_wl[b], S0 + i + 1)
                        for t in range(TILES):
                            bank = 2 if t == SAMPLE else t % 2
                            pe.wait_ge(s_xl, S0 + t + 1)
                            pe.wait_ge(s_sig, S0 + TILES * n + t + 1)
                            pe.sem_inc(s_open, 1)
                            for k in range(KC):
                                for xs, part in ((xh, upper[b]), (xh, lower[b]), (xl, upper[b])):
                                    ins = pe.matmul(ps[:, bank, :], xs[:, t, k, :], part[:, k, :],
                                                    start=(k == 0 and xs is xh and part is upper[b]), stop=(k == KC - 1 and xs is xl))
                            ins.then_inc(s_prod, 1)

            @block.scalar
            def _(act):
                act.sem_inc(s_sig, 2)
                act.wait_ge(ready, S0 + 16)
                copy = lambda dst, src: act.activation(dst, src, ACT.Copy)
                split_upper(copy, 0)
                for t in range(TILES):
                    act.wait_ge(s_x[t % X_RING], S0 + 16 * (t // X_RING + 1))
                    copy(xh[:, t], x[t % X_RING][:]).then_inc(s_xh, 1)
                with act.Fori(0, NG // 2) as i:
                    for b in range(2):
                        n = 2 * i + b

                        def sigmoid(t, bank, u):
                            act.wait_ge(s_prod, S0 + TILES * n + t + 1)
                            act.wait_ge(s_out[bank], S0 + 16 * uses(n, bank, u))
                            act.activation(g[:, bank, :], ps[:, bank, :], ACT.Sigmoid).then_inc(s_sig, 1)
                        over_tiles(act, sigmoid)

            @block.vector
            def _(dve):
                dve.wait_ge(s_wh[0], S0 + 1)
                split_lower(dve, 0)
                for t in range(TILES):
                    dve.wait_ge(s_xh, S0 + t + 1)
                    dve.tensor_tensor(xl[:, t], x[t % X_RING][:], xh[:, t].bitcast(F32), ALU.subtract).then_inc(s_xl, 1)
                s = Chain(dve, tap)
                for j in range(CT):
                    a, yj = c.aT[:, j, :], y[j]
                    s.link(dve.tensor_scalar(yj[:], a[:, 0:CONV_OUT], c.dw[:, j, 0:1], c.vec[:, V_BDW + j:V_BDW + j + 1],
                                             ALU.mult, ALU.add))
                    for k in range(1, CW):
                        ins = dve.scalar_tensor_tensor(yj[:], a[:, k:k + CONV_OUT], c.dw[:, j, k:k + 1], yj[:], ALU.mult, ALU.add)
                        if k == CW - 1:
                            ins.then_inc(y_done, 1)
                        else:
                            s.link(ins)


class Unit:

    def __init__(self, q_at, rows, k_at, keys, values, masked, out_tile):
        self.q_at, self.rows, self.k_at, self.keys = q_at, rows, k_at, keys
        self.values, self.masked, self.out_tile = values, masked, out_tile
        self.groups = [values[i:i + 4] for i in range(0, len(values), 4)]


SLOTS = 3


def attention(nc, c, tag, heads, K, dh, q_cols, k_cols, v_tiles, units, loads, out, ahead=None):
    scale = float(dh) ** -0.5
    U = len(units)
    n_groups = sum(len(u.groups) for u in units)
    assert 2 * U % SLOTS == 0 and max(len(u.groups) for u in units) <= 2
    with Phase(nc, tag) as p:
        qT = [p.sb(f"qT{b}", [K, q_cols]) for b in range(2)]
        kT = [p.sb(f"kT{b}", [K, k_cols]) for b in range(2)]
        v = [p.sb(f"v{b}", [P, v_tiles, dh]) for b in range(2)]
        probs = [p.sb(f"probs{b}", [P, 2 * BANK]) for b in range(SLOTS)]
        pT = [p.sb(f"probs_T{b}", [P, 8, P]) for b in range(SLOTS)]
        o = [p.sb(f"o{b}", [P, dh]) for b in range(SLOTS)]
        top, bias, total, inv = (p.sb(n, [P, SLOTS]) for n in ("row_max", "exp_bias", "row_sum", "row_scale"))
        S = [p.banks(f"scores{b}", 2) for b in range(SLOTS)]
        T = p.banks("turned", 1)
        O = p.banks("out", 1)
        s_in, s_head = p.sems("head_in_sbuf", 2), p.sems("head_done", 2)
        s_scores, s_max, s_bias, s_exp = (p.sems(n, SLOTS) for n in ("scored", "max", "bias", "exp"))
        s_turn, s_kept = p.sems("probs_turned", 2), p.sems("probs_T_kept", 2)
        s_pv, s_inv, s_o, s_out = (p.sems(n, SLOTS) for n in ("pv", "scale", "o", "o_stored"))
        s_open = p.sem("sample_opened")
        n_loads = len(loads(0, 0))

        class At:
            def __init__(self, i, b, m):
                w = b * U + m
                self.b, self.m, self.unit, self.slot, self.before = b, m, units[m], w % SLOTS, 2 * U // SLOTS * i + w // SLOTS
                g = b * n_groups + sum(len(u.groups) for u in units[:m])
                self.group = [((g + k) % 2, n_groups * i + (g + k) // 2) for k in range(len(self.unit.groups))]
                self.last_slot, self.last_use = (w - 1) % SLOTS, 2 * U // SLOTS * i + (w + SLOTS - 1) // SLOTS
                self.former = [((g + k - 1) % 2, n_groups * i + (g + k + 1) // 2) for k in range(len(self.unit.groups))]

        def line(i):
            return [At(i, b, m) for b in range(2) for m in range(U)]

        def turns(eng, first, rest):
            with eng.Fori(0, heads // 2) as i:
                units_of = line(i)
                for a in units_of[:2]:
                    first(i, a)
                for k, a in enumerate(units_of):
                    rest(i, a, units_of[k + 2] if k + 2 < len(units_of) else None)

        p.start()
        with nc.Block() as block:
            @block.tensor
            def _(pe):
                def score_bank(i, a, k):
                    u = a.unit
                    if k >= u.keys:
                        return
                    if k == 0:
                        if a.m == 0:
                            pe.wait_ge(s_in[a.b], S0 + 16 * n_loads * (i + 1))
                        pe.wait_ge(s_exp[a.slot], S0 + a.before)
                    n = min(BANK, u.keys - k)
                    last = k + n == u.keys
                    ins = pe.matmul(S[a.slot][0:u.rows, k // BANK, 0:n], qT[a.b][:, u.q_at:u.q_at + u.rows],
                                    kT[a.b][:, u.k_at + k:u.k_at + k + n], start=True, stop=not (last and u.masked))
                    if last and u.masked:
                        ins = pe.matmul(S[a.slot][0:u.rows, k // BANK, n - u.rows:n], c.ident[:, 0:u.rows],
                                        c.causal[:, 0:u.rows], start=False, stop=True)
                    if last:
                        ins.then_inc(s_scores[a.slot], 1)

                def scores(i, a):
                    for k in range(2):
                        score_bank(i, a, k * BANK)

                def rest(i, a, ahead):
                    u = a.unit
                    pe.wait_ge(s_exp[a.slot], S0 + a.before + 1)
                    for k in range(2):
                        if k < len(u.groups):
                            g, former, kept = a.group[k][0], *a.former[k]
                            pe.wait_ge(s_kept[former], S0 + kept)
                            if u.rows < P:
                                pe.sem_inc(s_open, 1)
                            for n, (vt, keys) in enumerate(u.groups[k]):
                                at = (vt - u.values[0][0]) * P
                                ins = pe.transpose(T[0:keys, 0, n * P:n * P + u.rows], probs[a.slot][0:u.rows, at:at + keys],
                                                   c.ident[0:u.rows, 0:u.rows])
                            ins.then_inc(s_turn[g], 1)
                        if ahead is not None:
                            score_bank(i, ahead, k * BANK)
                    pe.wait_ge(s_o[a.last_slot], S0 + a.last_use)
                    for (g, used), tiles in zip(a.group, u.groups):
                        pe.wait_ge(s_kept[g], S0 + used + 1)
                        if u.rows < P:
                            pe.sem_inc(s_open, 1)
                        for vt, keys in tiles:
                            k = vt - u.values[0][0]
                            ins = pe.matmul(O[0:u.rows, 0, a.slot * dh:(a.slot + 1) * dh], pT[a.slot][0:keys, k, 0:u.rows],
                                            v[a.b][0:keys, vt, :], start=(k == 0), stop=(k == len(u.values) - 1))
                    ins.then_inc(s_pv[a.slot], 1)
                    if a.m == U - 1:
                        pe.wait_ge(s_pv[a.slot], S0 + a.before + 1)
                        pe.sem_inc(s_head[a.b], 1)
                turns(pe, scores, rest)

            def keep(eng, copy, a, g_slot):
                u = a.unit
                for (g, used), tiles in zip(a.group, u.groups):
                    if g != g_slot:
                        continue
                    eng.wait_ge(s_turn[g], S0 + used + 1)
                    eng.wait_ge(s_pv[a.slot], S0 + a.before)
                    full = [t for t in tiles if t[1] == P]
                    k0 = tiles[0][0] - u.values[0][0]
                    ins = None
                    if full:
                        ins = copy(pT[a.slot][:, k0:k0 + len(full), 0:u.rows],
                                   T[:, 0, 0:len(full) * P].rearrange("p (k t) -> p k t", t=P)[:, :, 0:u.rows])
                    if len(full) < len(tiles):
                        n = tiles[-1][1]
                        k = len(full)
                        ins = copy(pT[a.slot][0:n, k0 + k, 0:u.rows], T[0:n, 0, k * P:k * P + u.rows])
                    ins.then_inc(s_kept[g], 1)

            @block.scalar
            def _(act):
                def exps(i, a):
                    u, s = a.unit, a.slot
                    act.wait_ge(s_bias[s], S0 + a.before + 1)
                    act.wait_ge(s_pv[s], S0 + a.before)
                    act.wait_ge(s_inv[s], S0 + a.before)
                    act.activation(probs[s][0:u.rows, 0:u.keys],
                                   S[s][0:u.rows, :, :].rearrange("p a n -> p (a n)")[:, 0:u.keys], ACT.Exp,
                                   bias=bias[0:u.rows, s:s + 1], scale=scale, accum_out=total[0:u.rows, s:s + 1]).then_inc(s_exp[s], 1)

                def rest(i, a, ahead):
                    keep(act, lambda dst, src: act.activation(dst, src, ACT.Copy), a, 0)
                    if ahead is not None:
                        exps(i, ahead)
                turns(act, exps, rest)

            @block.vector
            def _(dve):
                def maxes(i, a):
                    u, s = a.unit, a.slot
                    dve.wait_ge(s_scores[s], S0 + a.before + 1)
                    dve.tensor_reduce(top[0:u.rows, s:s + 1], S[s][0:u.rows, :, :].rearrange("p a n -> p (a n)")[:, 0:u.keys],
                                      AX, ALU.max).then_inc(s_max[s], 1)
                    dve.wait_ge(s_max[s], S0 + a.before + 1)
                    dve.wait_ge(s_exp[s], S0 + a.before)
                    dve.tensor_scalar(bias[0:u.rows, s:s + 1], top[0:u.rows, s:s + 1], -scale, None, ALU.mult).then_inc(s_bias[s], 1)

                def rest(i, a, ahead):
                    u, s = a.unit, a.slot
                    keep(dve, lambda dst, src: dve.tensor_copy(dst, src), a, 1)
                    if ahead is not None:
                        maxes(i, ahead)
                    dve.wait_ge(s_exp[s], S0 + a.before + 1)
                    dve.wait_ge(s_o[s], S0 + a.before)
                    dve.reciprocal(inv[0:u.rows, s:s + 1], total[0:u.rows, s:s + 1]).then_inc(s_inv[s], 1)
                    dve.wait_ge(s_inv[s], S0 + a.before + 1)
                    dve.wait_ge(s_pv[s], S0 + a.before + 1)
                    dve.wait_ge(s_out[s], S0 + 16 * a.before)
                    dve.tensor_scalar(o[s][0:u.rows, :], O[0:u.rows, 0, s * dh:(s + 1) * dh], inv[0:u.rows, s:s + 1], None, ALU.mult)\
                       .then_inc(s_o[s], 1)
                turns(dve, maxes, rest)

            @block.sync
            def _(sp):
                def store(i, a):
                    sp.wait_ge(s_o[a.slot], S0 + a.before + 1)
                    sp.dma_start(out[a.unit.out_tile, 0:a.unit.rows, bass.ts(2 * i + a.b, dh)], o[a.slot][0:a.unit.rows, :])\
                      .then_inc(s_out[a.slot], 16)
                def load(head, b):
                    for dst, src in loads(head, b):
                        buf = {"qT": qT, "kT": kT, "v": v}[dst[0]][b]
                        sp.dma_start(buf[dst[1:]] if len(dst) > 1 else buf[:], src).then_inc(s_in[b], 16)

                for b in range(2):
                    load(b, b)
                with sp.Fori(0, heads // 2 - 1) as i:
                    for a in line(i):
                        store(i, a)
                        if a.m == U - 1:
                            sp.wait_ge(s_head[a.b], S0 + i + 1)
                            load(2 * i + 2 + a.b, a.b)
                i = heads // 2 - 1
                for k, a in enumerate(line(i)):
                    store(i, a)
                    if ahead is not None and k % 2:
                        ahead.load(sp, 1)
                for s in range(SLOTS):
                    sp.wait_ge(s_out[s], S0 + 16 * (2 * U // SLOTS) * (heads // 2))


def forgetting_attention(nc, io, scr, c):
    n_past = PAST // P
    units = [Unit(t * P, P, 0, (t + 1) * P, [(j, P) for j in range(t + 1)], True, t) for t in range(NT)]
    units.append(Unit(SEQ, SAM, SEQ, PAST + SAM, [(NT + j, P) for j in range(n_past)] + [(NT + n_past, SAM)], True, SAMPLE))
    v_p = io["fox_v_prompt"][0, 0].rearrange("(t p) h d -> h p t d", p=P)
    v_c = io["cache_fox_v"][0, 0].rearrange("(t p) h d -> h p t d", p=P)
    v_s = io["fox_v_sample"][0, 0].rearrange("t h d -> h t d")
    every = slice(None)
    attention(nc, c, "fox", HF, DF + 2, DF, SEQ + SAM, SEQ + PAST + SAM, NT + n_past + 1, units, lambda h, b: [
        (("qT",), scr["qT"][h, :, 0:SEQ + SAM]), (("kT",), scr["kT"][h, :, 0:SEQ + PAST + SAM]),
        (("v", every, slice(0, NT)), v_p[h]), (("v", every, slice(NT, NT + n_past)), v_c[h]),
        (("v", slice(0, SAM), NT + n_past), v_s[h])], scr["fox"])


def memory_attention(nc, io, scr, c, ahead):
    M = NMEM // P
    units = [Unit(t * P, P, 0, NMEM, [(j, P) for j in range(M)], False, t) for t in range(NT)]
    units.append(Unit(SEQ, SAM, NMEM, NMEM, [(M + j, P) for j in range(M)], False, SAMPLE))
    v_p = io["mem_v_prompt"][0, 0].rearrange("(t p) h d -> h p t d", p=P)
    v_c = io["cache_mem_v"][0, 0].rearrange("(t p) h d -> h p t d", p=P)
    every = slice(None)
    attention(nc, c, "mem", HM, DM, DM, SEQ + SAM, 2 * NMEM, 2 * M, units, lambda h, b: [
        (("qT",), scr["mqT"][h, :, 0:SEQ + SAM]), (("kT", every, slice(0, NMEM)), scr["mkT"][0, h]),
        (("kT", every, slice(NMEM, 2 * NMEM)), scr["mkT"][1, h]),
        (("v", every, slice(0, M)), v_p[h]), (("v", every, slice(M, 2 * M)), v_c[h])], scr["mem"], ahead)


def merge(nc, io, scr, c, w, ahead):
    BK = DC // P
    with Phase(nc, "merge") as p:
        fox, mem, y, gates, m = ([p.sb(f"{n}{b}", shape) for b in range(2)] for n, shape in (
            ("fox", [P, DC]), ("mem", [P, DC]), ("y", [P, CT, P]), ("gates", [P, GATES]), ("merged", [P, D])))
        stats, mv, std, rstd = p.sb("ln_stats", [P, 6]), p.sb("ln_mean_var", [P, 2]), p.sb("ln_std", [P, 1]), p.sb("ln_scale", [P, 1])
        yn = p.sb("y_normed", [P, DC])
        turned = {n: p.sb(f"{n}_T", [P, BK, P]) for n in ("fox", "mem", "conv")}
        part = p.sb("gated_part", [P, D])
        pY, pF, pM, pN = (p.banks(n, 1) for n in ("y_rows", "fox_T", "mem_T", "yn_T"))
        pP = p.banks("products", 2)
        s_in, s_done, s_out = p.sems("tile_in_sbuf", 2), p.sems("tile_merged", 2), p.sems("tile_stored", 2)
        s_y, s_f, s_m, s_ynT = (p.sem(n) for n in ("y_turned", "fox_turned", "mem_turned", "yn_turned"))
        s_fk, s_mk, s_silu = (p.sem(n) for n in ("foxT_kept", "memT_kept", "silu"))
        s_ln, s_std, s_rstd, s_yn = p.sem("ln_step"), p.sem("ln_root"), p.sem("ln_scale"), p.sem("y_normed")
        s_prod, s_used, s_gate, s_open = p.sem("product"), p.sems("product_read", 2), p.sem("gate_step"), p.sem("opened")
        y_view = scr["y"].rearrange("j p t -> p j t")
        PRODS = 6

        p.start()
        with nc.Block() as block:
            @block.sync
            def _(sp):
                for buf, src in ((fox, scr["fox"][0]), (mem, scr["mem"][0]), (y, y_view[:, :, 0:P]), (gates, scr["gates"][0])):
                    sp.dma_start(buf[0][:], src).then_inc(s_in[0], 16)
                w.load(sp)

                def load(T):
                    n = SAM if T.sample else P
                    b = T.b
                    sp.wait_ge(s_done[b], S0 + T.u)
                    sp.dma_start(fox[b][0:n, :], scr["fox"][T.n, 0:n, :]).then_inc(s_in[b], 16)
                    sp.dma_start(mem[b][0:n, :], scr["mem"][T.n, 0:n, :]).then_inc(s_in[b], 16)
                    sp.dma_start(y[b][:, :, 0:n], y_view[:, :, SEQ + HIST:] if T.sample else y_view[:, :, bass.ts(T.n, P)])\
                        .then_inc(s_in[b], 16)
                    sp.dma_start(gates[b][0:n, :], scr["gates"][T.n, 0:n, :]).then_inc(s_in[b], 16)

                def emit(T):
                    n = SAM if T.sample else P
                    if not T.last:
                        load(T.next())
                    sp.wait_ge(s_done[T.b], S0 + T.u + 1)
                    sp.dma_start(scr["m"][T.n, 0:n, :], m[T.b][0:n, :]).then_inc(s_out[T.b], 16)
                    if T.sample:
                        sp.dma_start(scr["m"][T.n, n:P, :], m[T.b][0:n, :]).then_inc(s_out[T.b], 16)
                    if isinstance(T.u, int):
                        ahead.load(sp, KC)
                all_tiles(sp, emit)
                sp.wait_ge(s_out[0], S0 + 16 * (NT // 2 + 2))
                sp.wait_ge(s_out[1], S0 + 16 * (NT // 2))

            n_in = 4

            @block.tensor
            def _(pe):
                def turn_branches(T):
                    n, N = (SAM if T.sample else P), T.n
                    pe.wait_ge(s_in[T.b], S0 + 16 * n_in * (T.u + 1))
                    for src, bank, kept, done in ((fox, pF, s_fk, s_f), (mem, pM, s_mk, s_m)):
                        pe.wait_ge(kept, S0 + N)
                        for k in range(BK):
                            ins = pe.transpose(bank[:, 0, k * P:k * P + n], src[T.b][0:n, k * P:(k + 1) * P], c.ident[0:n, 0:n])
                        ins.then_inc(done, 1)
                    pe.wait_ge(s_yn, S0 + N)
                    for j in range(CT):
                        ins = pe.transpose(pY[0:n, 0, j * P:(j + 1) * P], y[T.b][:, j, 0:n], c.ident[:])
                    ins.then_inc(s_y, 1)

                def emit(T):
                    n, N = (SAM if T.sample else P), T.n
                    if T.b == 0:
                        for ready in w.ready.values():
                            pe.wait_ge(ready, S0 + 16)

                    def product(b, name, ready):
                        pe.wait_ge(ready, S0 + N + 1)
                        for h in range(2):
                            pe.wait_ge(s_used[h], S0 + 3 * N + b)
                            for k in range(BK):
                                ins = pe.matmul(pP[0:n, h, :], turned[name][:, k, 0:n], w.buf[f"w_{name}_o"][:, k, h * BANK:(h + 1) * BANK],
                                                start=(k == 0), stop=(k == BK - 1))
                            ins.then_inc(s_prod, 1)
                    product(0, "fox", s_fk)
                    pe.wait_ge(s_yn, S0 + N + 1)
                    pe.wait_ge(s_silu, S0 + N)
                    for k in range(BK):
                        ins = pe.transpose(pN[:, 0, k * P:k * P + n], yn[0:n, k * P:(k + 1) * P], c.ident[0:n, 0:n])
                    ins.then_inc(s_ynT, 1)
                    product(1, "mem", s_mk)
                    product(2, "conv", s_silu)
                    if not T.last:
                        turn_branches(T.next())
                turn_branches(Tile(0, 0))
                all_tiles(pe, emit)

            @block.scalar
            def _(act):
                def keep_branches(T):
                    n, N = (SAM if T.sample else P), T.n
                    for name, bank, ready, kept in (("fox", pF, s_f, s_fk), ("mem", pM, s_m, s_mk)):
                        act.wait_ge(ready, S0 + N + 1)
                        act.activation(turned[name][:, :, 0:n], bank[:, 0, :].rearrange("p (k t) -> p k t", t=P)[:, :, 0:n], ACT.Copy)\
                           .then_inc(kept, 1)
                    act.wait_ge(s_ln, S0 + 2 * N + 2)
                    act.wait_ge(s_yn, S0 + N)
                    act.activation(std[0:n, :], mv[0:n, 1:2], ACT.Sqrt, bias=c.eps[0:n, 0:1]).then_inc(s_std, 1)

                def emit(T):
                    n, N = (SAM if T.sample else P), T.n
                    act.wait_ge(s_ynT, S0 + N + 1)
                    act.wait_ge(s_prod, S0 + PRODS * N)
                    for k in range(BK):
                        ins = act.activation(turned["conv"][:, k, 0:n], pN[:, 0, k * P:k * P + n], ACT.Silu,
                                             scale=c.vec[:, V_LNW + k:V_LNW + k + 1], bias=c.vec[:, V_LNB + k:V_LNB + k + 1])
                    ins.then_inc(s_silu, 1)
                    if not T.last:
                        act.wait_ge(s_prod, S0 + PRODS * N + 4)
                        keep_branches(T.next())
                keep_branches(Tile(0, 0))
                all_tiles(act, emit)

            @block.vector
            def _(dve):
                def norm_y(T):
                    n, N = (SAM if T.sample else P), T.n
                    dve.wait_ge(s_y, S0 + N + 1)
                    dve.wait_ge(s_std, S0 + N)
                    dve.bn_stats(stats[0:n, :], pY[0:n, 0, :]).then_inc(s_ln, 1)
                    dve.wait_ge(s_ln, S0 + 2 * N + 1)
                    dve.sem_inc(s_open, 1)
                    dve.bn_aggr(mv[0:n, :], stats[0:n, :]).then_inc(s_ln, 1)
                    dve.wait_ge(s_std, S0 + N + 1)
                    dve.reciprocal(rstd[0:n, :], std[0:n, :]).then_inc(s_rstd, 1)
                    dve.wait_ge(s_rstd, S0 + N + 1)
                    dve.wait_ge(s_ynT, S0 + N)
                    dve.tensor_scalar(yn[0:n, :], pY[0:n, 0, :], mv[0:n, 0:1], rstd[0:n, 0:1], ALU.subtract, ALU.mult)\
                       .then_inc(s_yn, 1)

                def emit(T):
                    n, N, b = (SAM if T.sample else P), T.n, T.b
                    dve.wait_ge(s_in[b], S0 + 16 * n_in * (T.u + 1))
                    dve.wait_ge(s_out[b], S0 + 16 * T.u)
                    step = 10 * N
                    for br, (g_at, use) in enumerate(((0, 0), (2, 1), (1, 2))):
                        for h in range(2):
                            cols = slice(h * BANK, (h + 1) * BANK)
                            dst = m[b] if br == 0 else part
                            dve.wait_ge(s_prod, S0 + PRODS * N + 2 * br + h + 1)
                            ins = dve.tensor_tensor(dst[0:n, cols], pP[0:n, h, :],
                                                    gates[b][0:n, g_at * D + h * BANK:g_at * D + (h + 1) * BANK], ALU.mult)
                            ins.then_inc(s_gate, 1)
                            step = step + 1
                            dve.wait_ge(s_gate, S0 + step)
                            dve.sem_inc(s_used[h], 1)
                            if br:
                                dve.tensor_tensor(m[b][0:n, cols], m[b][0:n, cols], part[0:n, cols], ALU.add).then_inc(s_gate, 1)
                                step = step + 1
                                dve.wait_ge(s_gate, S0 + step)
                    dve.sem_inc(s_done[b], 1)
                    if not T.last:
                        norm_y(T.next())

                norm_y(Tile(0, 0))
                all_tiles(dve, emit)


U_RING, V_RING = 8, 8
ROUND = 2 * TOPK
GROUP = 2
DIAGS = 4
TURNS = NH // 2
OUT_STEP = 2
LAST_PART = 2 * KC // OUT_STEP
AHEAD_AT = 12


class Turn:

    def __init__(self, t, hp):
        self.sample = t is SAMPLE
        self.steps = TOPK // 2 if self.sample else TOPK
        self.number = TURNS * t + hp
        if self.sample:
            self.before = ROUND * TURNS * NT + 2 * self.steps * hp
            self.u_uses = ROUND // U_RING * TURNS * NT + 2 * self.steps // U_RING * hp
            self.v_uses = ROUND // V_RING * TURNS * NT + 2 * self.steps // V_RING * hp
            self.groups = ROUND // GROUP * TURNS * NT + 2 * self.steps // GROUP * hp
        else:
            B = self.number
            self.before, self.groups = ROUND * B, ROUND // GROUP * B
            self.u_uses, self.v_uses = ROUND // U_RING * B, ROUND // V_RING * B
        self.out = SAM if self.sample else P

    def done(self, q):
        return ROUND + self.before + self.steps * (q + 1)


def experts(nc, io, scr, c, w):
    with Phase(nc, "peer") as p:
        wq, w_out = w.buf["w_q"], w.buf["w_out"]
        keysT = p.sb("keys_T", [P, 2 * NH, NK])
        u = [p.sb(f"u_rows{k}", [P, D]) for k in range(U_RING)]
        v = [p.sb(f"v_rows{k}", [P, D]) for k in range(V_RING)]
        h2n, h2 = p.sb("h2_next", [P, D]), p.sb("h2", [P, D])
        mT, gain = p.sb("merged_T", [P, KC, P]), p.sb("norm2_gain", [P, D])
        ss, root, inv = p.sb("x2_sum", [P, 1]), p.sb("x2_root", [P, 1]), p.sb("x2_scale", [P, 1])
        h2T = p.sb("h2_next_T", [P, KC, P])
        x2, y = p.sb("x2", [P, D]), p.sb("y", [P, D])
        idx = p.sb("expert_idx", [P, 2, TOPK], U32)
        g = p.sb("expert_gate", [P, 2, TOPK])
        twins = p.sb("twin_identity", [P, SAM])
        twin_idx, twin_g = p.sb("twin_idx", [P, 2, TOPK // 2], U32), p.sb("twin_gate", [P, 2, TOPK // 2])
        dots, gl, wt = ([p.sb(f"{n}{q}", [P, TOPK]) for q in range(2)] for n in ("dots", "gelu", "weights"))
        diag = [p.sb(f"diag{k}", [P, P]) for k in range(DIAGS)]
        qs, qT = p.sb("q", [P, 2 * NK]), p.sb("q_T", [P, 2, P])
        sc, rep = p.sb("side_scores", [P, 2, NK]), p.sb("side_rest", [P, 2, NK])
        top, topi, topf = p.sb("side_top", [P, 2, TOPK]), p.sb("side_idx", [P, 2, TOPK], U32), p.sb("side_idx_f", [P, 2, TOPK])
        hot = p.sb("one_hot", [P, 2 * TOPK * TOPK])
        cand, crest = hot[:, 0:TOPK * TOPK], hot[:, TOPK * TOPK:]
        best, pos = p.sb("best", [P, TOPK]), p.sb("best_pos", [P, TOPK], U32)
        split, splitf = p.sb("pos_split", [P, 2, TOPK], U32), p.sb("pos_split_f", [P, 2, TOPK])
        pick = p.sb("picked", [P, 2 * TOPK])
        iota = p.sb("iota", [P, TOPK])
        ebias, ex, esum, einv = p.sb("exp_bias", [P, 1]), p.sb("exps", [P, TOPK]), p.sb("exp_sum", [P, 1]), p.sb("exp_scale", [P, 1])
        acc, pQ, pQT, pS, pH = p.banks("acc", 2), p.banks("q", 1), p.banks("q_T", 1), p.banks("scores", 1), p.banks("h2_T", 2)
        s_keys, s_kturn, s_kkeep, s_iota = (p.sem(n) for n in ("keys_in_sbuf", "keys_turned", "keysT_kept", "iota"))
        s_u, s_v = p.sems("u_gathered", U_RING, start=0), p.sems("v_gathered", V_RING, start=0)
        s_dot, s_sum, s_diag = p.sem("dots"), p.sem("sums"), p.sem("diagonals")
        s_gelu, s_wt = p.sem("gelu"), p.sem("weights")
        s_h2n, s_hcopy, s_hturn, s_hT = (p.sem(n) for n in ("h2_normed", "h2_copied", "h2_turned", "h2T_kept"))
        s_m, s_x, s_gain = p.sem("merged_in_sbuf"), p.sem("x_in_sbuf"), p.sem("gain_in_sbuf")
        s_mturn, s_mT, s_outp = p.sem("merged_turned"), p.sem("mergedT_kept"), p.sem("out_projected")
        s_sq, s_root, s_inv = p.sem("x2_squares"), p.sem("x2_root"), p.sem("x2_scale")
        s_x2, s_init, s_y, s_yout = (p.sem(n) for n in ("x2_summed", "sum_started", "y_rows", "y_stored"))
        s_q, s_qk, s_qt, s_qtk, s_sc = (p.sem(n) for n in ("q", "q_kept", "q_turned", "qT_kept", "side_scores"))
        s_route, s_eb, s_ex, s_done = (p.sem(n) for n in ("route_step", "exp_bias", "exps", "routed"))
        s_twins, s_parted = p.sem("twins"), p.sem("twins_parted")
        s_carry = p.sem("wait_carried")
        s_pcarry = p.sem("pool_wait_carried")
        ROUTE_AT = (0, 4, 6)
        ROUTE = 26
        x_p = io["x_prompt"][0].rearrange("(t p) d -> t p d", p=P)
        y_p = io["y_prompt"][0].rearrange("(t p) d -> t p d", p=P)

        def tiles(eng, start, queries, turn, end, ahead=lambda t, part: None):
            for part in range(LAST_PART + 1):
                ahead(0, part)
            queries(0)
            turn(None, 0, 0)
            with eng.Fori(0, NT) as t:
                start(t)
                with eng.Fori(0, TURNS - 2) as hp:
                    T = Turn(t, hp)
                    turn(T, 2 * T.number + 2, 2 * hp + 2)
                T = Turn(t, TURNS - 2)
                turn(T, 2 * T.number + 2, 2 * TURNS - 2, t + 1)
                queries(t + 1)
                T = Turn(t, TURNS - 1)
                turn(T, 2 * T.number + 2, 0)
                end(t)
            start(SAMPLE)
            with eng.Fori(0, TURNS - 1) as hp:
                T = Turn(SAMPLE, hp)
                turn(T, 2 * T.number + 2, 2 * hp + 2)
            turn(Turn(SAMPLE, TURNS - 1), None, None)
            end(SAMPLE)

        nothing = lambda t: None

        def sample_head(T, q):
            return 2 * (T.number - TURNS * NT) + q

        p.start()
        with nc.Block() as block:
            @block.sync
            def _(sp):
                for s, name in enumerate(("peer_keys1", "peer_keys2")):
                    sp.dma_start(u[s][:].rearrange("p (h d) -> p h d", h=NH), io[name][0].rearrange("h k d -> k h d")).then_inc(s_keys, 16)
                sp.dma_start(h2n[:], scr["m"][0]).then_inc(s_m, 16)
                w.load(sp)
                sp.dma_start(gain[:], io["norm2_w"][0].partition_broadcast(P)).then_inc(s_gain, 16)

                def load_x(halves):
                    for k, half in enumerate(halves):
                        sp.dma_start(x2[k * SAM:(k + 1) * SAM, :], half).then_inc(s_x, 16)
                load_x([x_p[0, 0:SAM, :], x_p[0, SAM:P, :]])

                def tile(t, x_next):
                    sp.wait_ge(s_hturn, S0 + t + 1)
                    sp.wait_ge(s_hcopy, S0 + t + 1)
                    sp.dma_start(h2n[:], scr["m"][t + 1]).then_inc(s_m, 16)
                    sp.wait_ge(s_init, S0 + t + 1)
                    load_x(x_next)
                    sp.wait_ge(s_y, S0 + t + 1)
                    sp.dma_start(y_p[t], y[:]).then_inc(s_yout, 16)
                with sp.Fori(0, NT - 1) as t:
                    tile(t, [x_p[t + 1, 0:SAM, :], x_p[t + 1, SAM:P, :]])
                tile(NT - 1, [io["x_sample"][0]] * 2)
                sp.wait_ge(s_y, S0 + NT + 1)
                sp.dma_start(io["y_sample"][0], y[0:SAM, :]).then_inc(s_yout, 16)
                sp.wait_ge(s_yout, S0 + 16 * (NT + 1))

            @block.gpsimd
            def _(pool):
                pool.iota(iota[:], pattern=[[1, TOPK]], base=0, channel_multiplier=0,
                          allow_small_or_imprecise_dtypes=True).then_inc(s_iota, 1)

                def turn(T, R, head, coming=None):
                    if T is None:
                        return
                    for q in range(2):
                        pool.wait_ge(s_done, S0 + 2 * T.number + q + 1)
                        if T.sample:
                            pool.wait_ge(s_parted, S0 + 4 * (sample_head(T, q) + 1))
                        rows = twin_idx if T.sample else idx
                        for j in range(T.steps):
                            at = T.steps * q + j
                            for rows_of, table, ring, used in ((u, "peer_u", s_u, s_dot), (v, "peer_v", s_v, s_sum)):
                                k = at % len(ring)
                                pool.wait_ge(used, S0 + ROUND + T.before + at - len(ring) + 1)
                                pool.sem_inc(s_pcarry, 1)
                                pool.indirect_dma_start(rows_of[k][:], None, io[table][0],
                                                        bass.IndirectOffsetOnAxis(ap=rows[:, q, j:j + 1], axis=0)).then_inc(ring[k], 16)
                pool.wait_ge(s_kturn, S0 + NH)
                tiles(pool, nothing, nothing, turn, nothing)

            @block.tensor
            def _(pe):
                for h in range(NH):
                    if h == 0:
                        pe.wait_ge(s_keys, S0 + 32)
                    if h >= 2:
                        pe.wait_ge(s_kkeep, S0 + h - 1)
                    for s in range(2):
                        ins = pe.transpose(pH[:, h % 2, s * P:(s + 1) * P], u[s][:, h * P:(h + 1) * P], c.ident[:])
                    ins.then_inc(s_kturn, 1)
                pe.wait_ge(s_kkeep, S0 + NH)
                for n in w.parts:
                    pe.wait_ge(w.ready[n], S0 + 16 * w.pieces)
                pe.sem_inc(s_sum, ROUND)

                def start(t):
                    rows = SAM if t is SAMPLE else P
                    pe.wait_ge(s_x2, S0 + t + 1)
                    pe.wait_ge(s_y, S0 + t)
                    for h in range(2):
                        ins = pe.matmul(acc[0:rows, h, :], c.ident[:, 0:rows], x2[:, h * BANK:(h + 1) * BANK],
                                        start=True, stop=True)
                    ins.then_inc(s_init, 1)

                def ahead(t, part):
                    if part == 0:
                        pe.wait_ge(s_m, S0 + 16 * (t + 1))
                        pe.wait_ge(s_hT, S0 + t)
                        for k in range(KC):
                            ins = pe.transpose(pH[:, k // 4, (k % 4) * P:(k % 4 + 1) * P], h2n[:, k * P:(k + 1) * P], c.ident[:])
                        ins.then_inc(s_mturn, 1)
                        return
                    if part == 1:
                        pe.wait_ge(s_mT, S0 + t + 1)
                    for n in range(OUT_STEP * (part - 1), OUT_STEP * part):
                        h, k = n // KC, n % KC
                        ins = pe.matmul(pH[:, h, :], mT[:, k, :], w_out[:, k, h * BANK:(h + 1) * BANK], start=(k == 0), stop=(k == KC - 1))
                    if part == LAST_PART:
                        ins.then_inc(s_outp, 1)

                def queries(t):
                    pe.wait_ge(s_h2n, S0 + t + 1)
                    for k in range(KC):
                        ins = pe.transpose(pH[:, k // 4, (k % 4) * P:(k % 4 + 1) * P], h2n[:, k * P:(k + 1) * P], c.ident[:])
                    ins.then_inc(s_hturn, 1)
                    pe.wait_ge(s_hT, S0 + t + 1)

                def route(R, head, part):
                    if part == 0:
                        pe.wait_ge(s_qk, S0 + R)
                        for k in range(KC):
                            ins = pe.matmul(pQ[:, 0, 0:2 * NK], h2T[:, k, :], wq[:, k, bass.ts(head, 2 * NK)],
                                            start=(k == 0), stop=(k == KC - 1))
                        ins.then_inc(s_q, 1)
                    elif part == 1:
                        pe.wait_ge(s_qk, S0 + R + 1)
                        pe.wait_ge(s_qtk, S0 + R)
                        for s in range(2):
                            ins = pe.transpose(pQT[:, 0, s * P:(s + 1) * P], qs[:, s * NK:(s + 1) * NK], c.ident[:])
                        ins.then_inc(s_qt, 1)
                    else:
                        pe.wait_ge(s_qtk, S0 + R + 1)
                        pe.wait_ge(s_done, S0 + R)
                        for s in range(2):
                            ins = pe.matmul(pS[:, 0, s * NK:(s + 1) * NK], qT[:, s, :],
                                            keysT[:, bass.ds(2 * head + s, 1), :].rearrange("p o k -> p (o k)"), start=True, stop=True)
                        ins.then_inc(s_sc, 1)

                def turn(T, R, head, coming=None):
                    for q in range(2):
                        if T is None:
                            for part in range(3):
                                route(R + q, head + q, part)
                            continue
                        for j in range(T.steps):
                            at = T.steps * q + j
                            if coming is not None and 0 <= at - AHEAD_AT <= LAST_PART:
                                ahead(coming, at - AHEAD_AT)
                            if R is not None and j in ROUTE_AT:
                                route(R + q, head + q, ROUTE_AT.index(j))
                            pe.wait_ge(s_diag, S0 + ROUND + T.before + at + 1)
                            pe.wait_ge(s_v[at % V_RING], 16 * (T.v_uses + at // V_RING + 1))
                            for h in range(2):
                                ins = pe.matmul(acc[0:T.out, h, :], diag[at % DIAGS][:, 0:T.out], v[at % V_RING][:, h * BANK:(h + 1) * BANK],
                                                start=False, stop=False, skip_group_check=True)
                            ins.then_inc(s_sum, 1)
                tiles(pe, start, queries, turn, nothing, ahead)

            @block.scalar
            def _(act):
                for h in range(NH):
                    act.wait_ge(s_kturn, S0 + h + 1)
                    act.activation(keysT[:, 2 * h:2 * h + 2, :], pH[:, h % 2, 0:2 * P].rearrange("p (s k) -> p s k", s=2), ACT.Copy)\
                       .then_inc(s_kkeep, 1)
                act.sem_inc(s_diag, ROUND)
                act.wait_ge(s_twins, S0 + 1)

                def ahead(t, part):
                    if part == 0:
                        act.wait_ge(s_mturn, S0 + t + 1)
                        act.wait_ge(s_outp, S0 + t)
                        act.activation(mT[:], pH[:].rearrange("p a (k t) -> p (a k) t", t=P), ACT.Copy).then_inc(s_mT, 1)
                    elif part == LAST_PART:
                        act.wait_ge(s_x2, S0 + t + 1)
                        act.wait_ge(s_inv, S0 + t)
                        act.activation(h2n[:], x2[:], ACT.Square, accum_out=ss[:]).then_inc(s_sq, 1)
                        act.wait_ge(s_sq, S0 + t + 1)
                        act.activation(root[:], ss[:], ACT.Sqrt, scale=1.0 / D, bias=c.eps[:, 0:1]).then_inc(s_root, 1)

                def queries(t):
                    act.wait_ge(s_hturn, S0 + t + 1)
                    act.wait_ge(s_q, S0 + NH * t)
                    act.activation(h2T[:], pH[:].rearrange("p a (k t) -> p (a k) t", t=P), ACT.Copy).then_inc(s_hT, 1)

                def route(R, part):
                    if part == 0:
                        act.wait_ge(s_q, S0 + R + 1)
                        act.wait_ge(s_qt, S0 + R)
                        act.activation(qs[:], pQ[:, 0, 0:2 * NK], ACT.Copy).then_inc(s_qk, 1)
                    elif part == 1:
                        act.wait_ge(s_qt, S0 + R + 1)
                        act.wait_ge(s_sc, S0 + R)
                        act.activation(qT[:], pQT[:, 0, 0:2 * P].rearrange("p (s t) -> p s t", s=2), ACT.Copy).then_inc(s_qtk, 1)
                    else:
                        act.wait_ge(s_eb, S0 + R + 1)
                        act.wait_ge(s_done, S0 + R)
                        act.activation(ex[:], best[:], ACT.Exp, bias=ebias[:, 0:1], accum_out=esum[:]).then_inc(s_ex, 1)

                def turn(T, R, head, coming=None):
                    for q in range(2):
                        if T is None:
                            for part in range(3):
                                route(R + q, part)
                            continue
                        for k in range(T.steps // GROUP):
                            at = T.steps * q + GROUP * k
                            cols = slice(GROUP * k, GROUP * (k + 1))
                            act.wait_ge(s_dot, S0 + ROUND + T.before + at + GROUP)
                            act.activation(gl[q][:, cols], dots[q][:, cols], ACT.Gelu).then_inc(s_gelu, 1)
                            act.wait_ge(s_wt, S0 + T.groups + T.steps // GROUP * q + k + 1)
                            for j in range(GROUP):
                                act.wait_ge(s_sum, S0 + ROUND + T.before + at + j - DIAGS + 1)
                                eye = twins[:] if T.sample else c.ident[:]
                                act.activation(diag[(at + j) % DIAGS][:, 0:T.out], eye, ACT.Copy,
                                               scale=wt[q][:, GROUP * k + j:GROUP * k + j + 1]).then_inc(s_diag, 1)
                            if coming is not None and at <= AHEAD_AT < at + GROUP:
                                ahead(coming, 0)
                            if R is not None and k < 2:
                                route(R + q, k)
                        if coming is not None and q:
                            ahead(coming, LAST_PART)
                        if R is not None:
                            route(R + q, 2)

                def end(t):
                    rows = SAM if t is SAMPLE else P
                    done = ROUND * TURNS * (t + 1) if t is not SAMPLE else ROUND * TURNS * NT + TOPK * TURNS
                    act.wait_ge(s_sum, S0 + ROUND + done)
                    act.wait_ge(s_yout, S0 + 16 * t)
                    act.activation(y[0:rows, :], acc[0:rows, :, :].rearrange("p a n -> p (a n)"), ACT.Copy).then_inc(s_y, 1)
                tiles(act, nothing, queries, turn, end, ahead)

            @block.vector
            def _(dve):
                dve.sem_inc(s_dot, ROUND)
                dve.wait_ge(s_iota, S0 + 1)

                dve.tensor_tensor(twins[:], c.ident[:, 0:SAM], c.ident[:, SAM:P], ALU.add).then_inc(s_twins, 1)

                def start(t):
                    dve.wait_ge(s_dot, S0 + ROUND + ROUND * TURNS * t)
                    dve.wait_ge(s_h2n, S0 + t + 1)
                    dve.tensor_copy(h2[:], h2n[:]).then_inc(s_hcopy, 1)
                    if t is SAMPLE:
                        for q in range(2):
                            part(q, q)
                    dve.wait_ge(s_hcopy, S0 + t + 1)
                    carry()

                def carry():
                    dve.sem_inc(s_carry, 1)

                def route(R, q, former):
                    s = Chain(dve, s_route)
                    s.n = ROUTE * R
                    dve.wait_ge(s_sc, S0 + R + 1)
                    s.link(dve.tensor_copy(sc[:], pS[:, 0, 0:2 * NK].rearrange("p (s k) -> p s k", s=2)))
                    carry()
                    for i in range(2):
                        s.step(dve.max(top[:, i, 0:8], sc[:, i, :]))
                    s.wait()
                    carry()
                    for i in range(2):
                        s.step(dve.match_replace(rep[:, i, :], top[:, i, 0:8], sc[:, i, :], LOWEST))
                        s.step(dve.max_index(topi[:, i, 0:8], top[:, i, 0:8], sc[:, i, :]))
                    s.wait()
                    carry()
                    for i in range(2):
                        s.step(dve.max(top[:, i, 8:16], rep[:, i, :]))
                    s.wait()
                    carry()
                    for i in range(2):
                        s.step(dve.max_index(topi[:, i, 8:16], top[:, i, 8:16], rep[:, i, :]))
                    sq = lambda ap: ap.rearrange("p (a b) -> p a b", a=TOPK)
                    s.wait()
                    s.step(dve.tensor_copy(topf[:], topi[:]))
                    s.link(dve.tensor_tensor(sq(cand), top[:, 0, :].unsqueeze(2).broadcast_to([P, TOPK, TOPK]),
                                             top[:, 1, :].unsqueeze(1).broadcast_to([P, TOPK, TOPK]), ALU.add))
                    carry()
                    s.link(dve.max(best[:, 0:8], cand))
                    carry()
                    s.step(dve.match_replace(crest, best[:, 0:8], cand, LOWEST))
                    s.link(dve.max_index(pos[:, 0:8], best[:, 0:8], cand))
                    carry()
                    s.step(dve.max(best[:, 8:16], crest))
                    dve.tensor_scalar(ebias[:], best[:, 0:1], -1.0, None, ALU.mult).then_inc(s_eb, 1)
                    s.wait()
                    carry()
                    s.link(dve.max_index(pos[:, 8:16], best[:, 8:16], crest))
                    s.step(dve.tensor_scalar(split[:, 0, :], pos[:], 4, None, ALU.logical_shift_right))
                    s.link(dve.tensor_scalar(split[:, 1, :], pos[:], TOPK - 1, None, ALU.bitwise_and))
                    s.link(dve.tensor_copy(splitf[:], split[:]))
                    flat = splitf[:].rearrange("p s j -> p (s j)")
                    s.link(dve.tensor_tensor(hot[:].rearrange("p (m a) -> p m a", a=TOPK), flat.unsqueeze(2).broadcast_to([P, 2 * TOPK, TOPK]),
                                             iota[:].unsqueeze(1).broadcast_to([P, 2 * TOPK, TOPK]), ALU.is_equal))
                    hot4 = hot[:].rearrange("p (s j a) -> p s j a", s=2, a=TOPK)
                    s.link(dve.tensor_tensor(hot4, hot4, topf[:].unsqueeze(2).broadcast_to([P, 2, TOPK, TOPK]), ALU.mult))
                    s.link(dve.tensor_reduce(pick[:], hot[:].rearrange("p (m a) -> p m a", a=TOPK), AX, ALU.add))
                    if former is not None:
                        dve.wait_ge(s_sum, S0 + former.done(q))
                    s.step(dve.scalar_tensor_tensor(idx[:, q, :], pick[:, 0:TOPK], float(NK), pick[:, TOPK:], ALU.mult, ALU.add))
                    dve.wait_ge(s_ex, S0 + R + 1)
                    s.link(dve.reciprocal(einv[:], esum[:]))
                    dve.tensor_scalar(g[:, q, :], ex[:], einv[:, 0:1], None, ALU.mult).then_inc(s_done, 1)
                    assert s.taken == ROUTE, s.taken

                def part(n, q):
                    dve.wait_ge(s_done, S0 + 2 * TURNS * NT + n + 1)
                    half = TOPK // 2
                    for dst, src in ((twin_idx, idx), (twin_g, g)):
                        dve.tensor_copy(dst[0:SAM, q, :], src[0:SAM, q, 0:half]).then_inc(s_parted, 1)
                        dve.tensor_copy(dst[SAM:P, q, :], src[SAM:P, q, half:]).then_inc(s_parted, 1)

                def ahead(t, part):
                    if part != LAST_PART:
                        return
                    dve.wait_ge(s_x, S0 + 32 * (t + 1))
                    dve.wait_ge(s_outp, S0 + t + 1)
                    dve.tensor_tensor(x2[:], pH[:].rearrange("p a n -> p (a n)"), x2[:], ALU.add).then_inc(s_x2, 1)
                    dve.wait_ge(s_root, S0 + t + 1)
                    dve.reciprocal(inv[:], root[:]).then_inc(s_inv, 1)
                    dve.wait_ge(s_inv, S0 + t + 1)
                    dve.scalar_tensor_tensor(h2n[:], x2[:], inv[:, 0:1], gain[:], ALU.mult, ALU.mult).then_inc(s_h2n, 1)

                def turn(T, R, head, coming=None):
                    for q in range(2):
                        if T is not None:
                            gates = twin_g if T.sample else g
                            if T.sample:
                                dve.wait_ge(s_parted, S0 + 4 * (sample_head(T, q) + 1))
                            else:
                                dve.wait_ge(s_done, S0 + 2 * T.number + q + 1)
                            for j in range(T.steps):
                                at = T.steps * q + j
                                k = at % U_RING
                                dve.wait_ge(s_u[k], 16 * (T.u_uses + at // U_RING + 1))
                                dve.tensor_tensor_reduce(u[k][:], u[k][:], h2[:], 1.0, 0.0, ALU.mult, ALU.add,
                                                         dots[q][:, j:j + 1]).then_inc(s_dot, 1)
                                if j % GROUP == GROUP - 1:
                                    n = j // GROUP
                                    cols = slice(GROUP * n, GROUP * (n + 1))
                                    dve.wait_ge(s_gelu, S0 + T.groups + T.steps // GROUP * q + n + 1)
                                    dve.tensor_tensor(wt[q][:, cols], gl[q][:, cols], gates[:, q, cols], ALU.mult).then_inc(s_wt, 1)
                        if coming is not None and q:
                            ahead(coming, LAST_PART)
                            carry()
                        if R is not None:
                            route(R + q, q, T)
                            if T is not None and T.sample:
                                carry()
                                part(sample_head(T, q) + 2, q)
                dve.wait_ge(s_gain, S0 + 16)
                tiles(dve, start, nothing, turn, nothing, ahead)


OUTS = (("y_prompt", (1, SEQ, D)), ("y_sample", (1, SAM, D)),
        ("fox_k_prompt", (1, 1, SEQ, HF, DF)), ("fox_v_prompt", (1, 1, SEQ, HF, DF)), ("fox_logf_prompt", (1, 1, SEQ, HF)),
        ("conv_prompt", (1, 1, HIST, DC)),
        ("mem_k_prompt", (1, 1, NMEM, HM, DM)), ("mem_v_prompt", (1, 1, NMEM, HM, DM)),
        ("fox_k_sample", (1, 1, SAM, HF, DF)), ("fox_v_sample", (1, 1, SAM, HF, DF)), ("fox_logf_sample", (1, 1, SAM, HF)),
        ("conv_sample", (1, 1, HIST, DC)))


class Constants:
    pass


def build(nc, io, phases=99):
    scr = {name: nc.dram_tensor(f"scr_{name}", shape, F32).ap() for name, shape in (
        ("xT", (NT + 1, P, D)), ("qT", (HF, DF + 2, TOK)), ("kT", (HF, DF + 2, PAST + TOK)),
        ("mqT", (HM, DM, TOK)), ("mkT", (2, HM, DM, NMEM)), ("a", (TOK, DC)), ("gates", (NT + 1, P, GATES)),
        ("y", (CT, P, CONV_OUT)), ("fox", (NT + 1, P, HF * DF)), ("mem", (NT + 1, P, HM * DM)),
        ("m", (NT + 1, P, D)))}
    with ExitStack() as stack:
        c = Constants()
        c.ident = stack.enter_context(nc.sbuf_tensor("identity", [P, P], F32))
        c.vec = stack.enter_context(nc.sbuf_tensor("feature_vectors", [P, V_ROWS], F32))
        c.causal = stack.enter_context(nc.sbuf_tensor("causal_mask", [P, P], F32))
        c.eps = stack.enter_context(nc.sbuf_tensor("eps", [P, 1], F32))
        front(nc, io, scr, c, phases)
        if phases > 4:
            forgetting_attention(nc, io, scr, c)
            with Phase(nc, "w_peer") as pe:
                w_peer = Weights(pe, {"w_out": io["w_out"][0], "w_q": io["peer_w_q"][0]}, pieces=KC)
                with Phase(nc, "w_merge") as pw:
                    w_merge = Weights(pw, {n: io[n][0] for n in ("w_fox_o", "w_mem_o", "w_conv_o")})
                    memory_attention(nc, io, scr, c, w_merge)
                    if phases > 5:
                        merge(nc, io, scr, c, w_merge, w_peer)
                if phases > 6:
                    experts(nc, io, scr, c, w_peer)


def front(nc, io, scr, c, phases):
    with ExitStack() as stack:
        c.aT = stack.enter_context(nc.sbuf_tensor("conv_input_T", [P, CT, 2 * HIST + SEQ + SAM], F32))
        c.dw = stack.enter_context(nc.sbuf_tensor("conv_taps", [P, CT, CW], F32))
        c.forget = stack.enter_context(nc.sbuf_tensor("forget_logits", [P, NT + 1, HF], F32))
        constants(nc, io, scr, c)
        rows = lambda name: io[name].rearrange("l b (t p) h d -> (l b t) p (h d)", p=P)
        mem_k, mem_v = rows("mem_k_prompt"), rows("mem_v_prompt")
        mem_x = io["mem_prompt"][0].rearrange("(t p) d -> t p d", p=P)
        x_p = io["x_prompt"][0].rearrange("(t p) d -> t p d", p=P)
        k_p, v_p = rows("fox_k_prompt"), rows("fox_v_prompt")
        k_s, v_s = (io[n][0, 0].rearrange("t h d -> t (h d)") for n in ("fox_k_sample", "fox_v_sample"))
        a_t = scr["a"].rearrange("(t p) n -> t p n", p=P)
        heads_T = lambda name, at: scr[name][:, 0:DF, at].rearrange("h d t -> d h t")
        F = HF * DF
        kv_chunks = [
            Chunk("mk", "norm", 0, 0, HM * DM, head=DM, gain=io["mem_k_norm"][0], rows_out=lambda T: mem_k[T.n],
                  turn=P, turned_out=lambda T: scr["mkT"][0, :, :, bass.ts(T.n, P)].rearrange("h d t -> d h t")),
            Chunk("mv", "copy", 1, HM * DM, HM * DM, rows_out=lambda T: mem_v[T.n])]
        in_chunks = [
            Chunk("q", "norm", 0, 0, F, head=DF, gain=io["fox_q_norm"][0], turn=DF,
                  turned_out=lambda T: heads_T("qT", bass.ts(T.n, P))),
            Chunk("k", "norm", 1, F, F, head=DF, gain=io["fox_k_norm"][0], rows_out=lambda T: k_s if T.sample else k_p[T.n], turn=DF,
                  turned_out=lambda T: heads_T("kT", slice(SEQ + PAST, SEQ + PAST + P) if T.sample else bass.ts(T.n, P))),
            Chunk("mq", "norm", 2, C_MQ, HM * DM, head=DM, gain=io["mem_q_norm"][0], turn=P,
                  turned_out=lambda T: scr["mqT"][:, :, bass.ts(T.n, P)].rearrange("h d t -> d h t")),
            Chunk("v", "copy", 0, 2 * F, F, rows_out=lambda T: v_s if T.sample else v_p[T.n]),
            Chunk("ga", "glu", 1, C_GLU, DC, rows_out=lambda T: a_t[T.n][0:SAM] if T.sample else a_t[T.n], turn=P),
            Chunk("gb", "glu_gate", 2, C_GLU + DC, DC),
            Chunk("f", "forget", 0, 3 * F, HF)]
        parts = lambda weights, chunks: {ch.name: weights[:, ch.src:ch.src + ch.width] for ch in chunks}
        with Phase(nc, "w_in") as pw:
            w_in = Weights(pw, parts(io["w_in"][0], in_chunks))
            with Phase(nc, "w_kv") as pk:
                w_kv = Weights(pk, parts(io["w_mem_kv"][0], kv_chunks))
                project(nc, c, "memkv", lambda T: mem_x[T.n], V_MEMNORM, w_kv, kv_chunks, memory_tiles, ahead=w_in)
            if phases < 2:
                return
            project(nc, c, "in", lambda T: io["x_sample"][0] if T.sample else x_p[T.n], V_NORM1, w_in, in_chunks, all_tiles,
                    xT_out=lambda T: scr["xT"][T.n], forget=c.forget,
                    a_cols=lambda T: (c.aT[:, :, 2 * HIST + SEQ:] if T.sample else c.aT[:, :, bass.ds(HIST + T.n * P, P)]))
        if phases < 3:
            return
        with Phase(nc, "w_gates") as pw:
            w_gates = Weights(pw, {"gates": io["w_in"][0, :, C_G:C_G + BANK]})
            decay(nc, io, scr, c, w_gates)
            gates_and_conv(nc, io, scr, c, w_gates)


INS = ("x_prompt", "x_sample", "mem_prompt", "cache_fox_k", "cache_fox_v", "cache_fox_logf", "cache_conv",
       "cache_mem_k", "cache_mem_v", "norm1_w", "w_in", "b_forget", "fox_q_norm", "fox_k_norm", "w_fox_o",
       "w_dw", "b_dw", "conv_ln_w", "conv_ln_b", "w_conv_o", "mem_norm_w", "w_mem_kv", "mem_q_norm", "mem_k_norm",
       "w_mem_o", "w_out", "norm2_w", "peer_w_q", "peer_keys1", "peer_keys2", "peer_u", "peer_v")


def kernel(**inputs):
    import numpy as _np
    import concourse.bacc as _bacc
    from concourse import mybir as _mybir
    from concourse.bass_utils import run_bass_kernel_spmd as _run

    nc = _bacc.Bacc("TRN2", target_bir_lowering=False, num_devices=1)
    arrays, io = {}, {}
    for name in INS:
        a = _np.ascontiguousarray(inputs[name])
        arrays[f"in_{name}"] = a
        io[name] = nc.dram_tensor(f"in_{name}", a.shape, _mybir.dt.from_np(a.dtype), kind="ExternalInput").ap()
    for name, shape in OUTS:
        io[name] = nc.dram_tensor(f"out_{name}", shape, F32, kind="ExternalOutput").ap()
    build(nc, io)
    r = _run(nc, [arrays], core_ids=[0])
    return tuple(r.results[0][f"out_{name}"] for name, _ in OUTS)
```
